# Optimizing a Trainium2 kernel written in Bass

```python
import jax, jax.numpy as jnp
from jax import lax
import numpy as np

D_MODEL = 1024
BATCH = 1
SEQ = 2048
DEPTH = 1

CHUNK = 128
A_GROUPS = 8
A_GROUP_DIM = D_MODEL // A_GROUPS
A_WIDTH = A_GROUPS * A_GROUP_DIM
B_HEADS = 8
B_HEAD_DIM = D_MODEL // B_HEADS
B_WIDTH = B_HEADS * B_HEAD_DIM
Q_BLOCK = 128
EPS = 1e-6

IN_WIDTHS = (A_WIDTH, A_WIDTH, A_WIDTH, B_WIDTH, B_WIDTH, B_WIDTH, B_WIDTH, D_MODEL, D_MODEL)
IN_PROJ_WIDTH = sum(IN_WIDTHS)
SPLIT_POINTS = tuple(int(p) for p in np.cumsum(IN_WIDTHS)[:-1])

kernel_name = "hybrid_gmlp_stickbreaking_gated_block"

def rms_norm(x, gain):
    xf = x.astype(jnp.float32)
    y = xf * lax.rsqrt(jnp.mean(xf * xf, axis=-1, keepdims=True) + EPS)
    return (y * gain.astype(jnp.float32)).astype(x.dtype)

def chunked_spatial_gating(u, v, w_s, b_s):
    bsz, seq, _ = u.shape
    n_chunks = seq // CHUNK
    vr = v.reshape(bsz, n_chunks, CHUNK, A_GROUPS, A_GROUP_DIM)
    causal = jnp.tril(jnp.ones((CHUNK, CHUNK), dtype=bool))
    w = jnp.where(causal[None], w_s, 0.0).astype(v.dtype)
    mixed = jnp.einsum('gts,bnsgc->bntgc', w, vr)
    mixed = mixed + b_s.T.astype(v.dtype)[None, None, :, :, None]
    return u * mixed.reshape(bsz, seq, A_WIDTH)

def stick_breaking_attention(q, k, v):
    bsz, seq, n_heads, head_dim = q.shape
    n_blocks = seq // Q_BLOCK
    scale = head_dim ** -0.5
    q_blocks = q.reshape(bsz, n_blocks, Q_BLOCK, n_heads, head_dim).transpose(1, 0, 2, 3, 4)
    key_pos = jnp.arange(seq)

    def one_block(args):
        q_blk, blk_idx = args
        logits = jnp.einsum('bthd,bshd->bhts', q_blk, k).astype(jnp.float32) * scale
        q_pos = blk_idx * Q_BLOCK + jnp.arange(Q_BLOCK)
        causal = key_pos[None, :] < q_pos[:, None]
        log_beta = jax.nn.log_sigmoid(logits)
        log_one_minus = jnp.where(causal, log_beta - logits, 0.0)
        suffix = lax.cumsum(log_one_minus, axis=3, reverse=True) - log_one_minus
        weights = jnp.where(causal, jnp.exp(log_beta + suffix), 0.0)
        return jnp.einsum('bhts,bshd->bthd', weights.astype(v.dtype), v)

    out = lax.map(one_block, (q_blocks, jnp.arange(n_blocks)))
    return out.transpose(1, 0, 2, 3, 4).reshape(bsz, seq, n_heads, head_dim)

def setup_inputs(seed: int = 0) -> dict:
    key = jax.random.key(seed)
    ks = jax.random.split(key, 11)
    f32 = jnp.float32
    x = jax.random.normal(ks[0], (BATCH, SEQ, D_MODEL), f32)
    norm_in = 1.0 + 0.02 * jax.random.normal(ks[1], (DEPTH, D_MODEL), f32)
    w_in = jax.random.normal(ks[2], (DEPTH, D_MODEL, IN_PROJ_WIDTH), f32) * D_MODEL ** -0.5
    norm_v = 1.0 + 0.02 * jax.random.normal(ks[3], (DEPTH, A_WIDTH), f32)
    w_s = jax.random.normal(ks[4], (DEPTH, A_GROUPS, CHUNK, CHUNK), f32) * (0.5 * CHUNK ** -0.5)
    b_s = 1.0 + 0.02 * jax.random.normal(ks[5], (DEPTH, A_GROUPS, CHUNK), f32)
    w_o_gmlp = jax.random.normal(ks[6], (DEPTH, A_WIDTH, D_MODEL), f32) * A_WIDTH ** -0.5
    w_o_sb = jax.random.normal(ks[7], (DEPTH, B_WIDTH, D_MODEL), f32) * B_WIDTH ** -0.5
    w_out = jax.random.normal(ks[8], (DEPTH, D_MODEL, D_MODEL), f32) * D_MODEL ** -0.5
    norm_final = 1.0 + 0.02 * jax.random.normal(ks[9], (D_MODEL,), f32)
    return {"x": x, "norm_in": norm_in, "w_in": w_in, "norm_v": norm_v, "w_s": w_s,
            "b_s": b_s, "w_o_gmlp": w_o_gmlp, "w_o_sb": w_o_sb, "w_out": w_out,
            "norm_final": norm_final}

def reference(x, norm_in, w_in, norm_v, w_s, b_s, w_o_gmlp, w_o_sb, w_out, norm_final):
    bsz, seq, _ = x.shape
    for layer in range(DEPTH):
        h = rms_norm(x, norm_in[layer])
        proj = jnp.einsum('bsd,de->bse', h, w_in[layer])
        u_a, v_a, z_a, q_b, k_b, v_b, z_b, gate_a, gate_b = jnp.split(proj, SPLIT_POINTS, axis=-1)

        u_a = jax.nn.gelu(u_a)
        v_a = rms_norm(jax.nn.gelu(v_a), norm_v[layer])
        y_a = chunked_spatial_gating(u_a, v_a, w_s[layer], b_s[layer]) * jax.nn.silu(z_a)

        heads = lambda t: t.reshape(bsz, seq, B_HEADS, B_HEAD_DIM)
        y_b = stick_breaking_attention(heads(q_b), heads(k_b), heads(v_b)).reshape(bsz, seq, B_WIDTH)
        y_b = y_b * jax.nn.silu(z_b)

        p_a = jnp.einsum('bse,ed->bsd', y_a, w_o_gmlp[layer])
        p_b = jnp.einsum('bse,ed->bsd', y_b, w_o_sb[layer])
        merged = jax.nn.sigmoid(gate_a) * p_a + jax.nn.sigmoid(gate_b) * p_b
        x = x + jnp.einsum('bsd,de->bse', merged, w_out[layer])
    return rms_norm(x, norm_final)


_drawn_inputs = setup_inputs


def setup_inputs(seed=0):
    import zlib

    import numpy as np

    out = dict(_drawn_inputs(seed))
    spreads = {}
    factors = {'norm_in': 5.694, 'norm_v': 8.0, 'b_s': 8.0, 'norm_final': 2.849}
    for name, (base, spread) in spreads.items():
        noise = np.random.default_rng([zlib.crc32(name.encode()), seed]).standard_normal(out[name].shape)
        drawn = base * np.exp(spread * noise) if base else spread * noise
        out[name] = __import__('jax').numpy.asarray(drawn.astype(out[name].dtype))
    for name, factor in factors.items():
        out[name] = (out[name] * factor).astype(out[name].dtype)
    return out
```

```python
from contextlib import ExitStack

import concourse.bass as bass
from concourse import mybir
from concourse.alu_op_type import AluOpType as ALU

ACT = mybir.ActivationFunctionType
F32 = mybir.dt.float32
F32R = mybir.dt.float32r

P = 128
D = 1024
S = 2048
KT = D // P
NT = S // P
CW = 512
NC = S // CW
HEADS = 8
GROUPS = 8
EPS = 1e-6
SCALE = float(P) ** -0.5
MASKED = -1e30
WT = 2 * P
BANKS = 8


class Scope:

    def __init__(self, nc, memory, prefix):
        self.nc, self.memory, self.prefix, self.used = nc, memory, prefix, []

    def clear(self):
        self.nc.clear_and_free_semaphores(self.used)
        self.nc.all_engine_barrier()

    def sb(self, name, shape, dt=F32):
        return self.memory.enter_context(self.nc.sbuf_tensor(f"{self.prefix}_{name}", shape, dt))

    def ps(self, name, shape):
        return self.memory.enter_context(self.nc.psum_tensor(f"{self.prefix}_{name}", shape, F32))

    def sem(self, name):
        self.used.append(self.nc.alloc_semaphore(name=f"{self.prefix}_{name}"))
        return self.used[-1]

    def sems(self, name, n):
        return [self.sem(f"{name}{i}") for i in range(n)]


def wait_past(eng, sem, count):
    if not (isinstance(count, int) and count == 0):
        eng.wait_ge(sem, count)


def turns_from_first(eng, turns, body):
    body(0)
    with eng.Fori(1, turns) as t:
        body(t)


class Projection:

    def __init__(self, sc, act_hi, act_lo, banks):
        self.act_hi, self.act_lo, self.banks = act_hi, act_lo, banks
        self.stage = sc.sb("w_stage", [P, 2, KT, WT])
        self.w_hi = sc.sb("w_hi", [P, 2, KT, WT], F32R)
        self.w_lo = sc.sb("w_lo", [P, 2, KT, WT], F32R)
        self.w_loaded = sc.sems("w_loaded", 2)
        self.hi_split = sc.sems("hi_split", 2)
        self.w_ready = sc.sems("w_ready", 2)
        self.full = [sc.sems(f"full{b}_", BANKS) for b in range(2)]
        self.free = sc.sems("free", BANKS)

    def start(self, reader):
        for i in range(BANKS):
            reader.sem_inc(self.free[i], 1)

    def load(self, sp, turn, b, pieces):
        wait_past(sp, self.w_ready[b], turn)
        for dst, src in pieces:
            sp.dma_start(dst, src).then_inc(self.w_loaded[b], 16)

    def by_rows(self, b, weights, at):
        return [(self.stage[:, b, h * KT // 2:(h + 1) * KT // 2, :],
                 weights[:, h * KT // 2:(h + 1) * KT // 2, bass.ds(at, WT)]) for h in range(2)]

    def split(self, dve, turn, b):
        dve.wait_ge(self.w_loaded[b], 32 * turn + 32)
        wait_past(dve, self.full[b][BANKS - 1], turn)
        dve.tensor_copy(self.w_hi[:, b], self.stage[:, b]).then_inc(self.hi_split[b], 1)
        dve.wait_ge(self.hi_split[b], turn + 1)
        dve.tensor_tensor(self.w_lo[:, b], self.stage[:, b], self.w_hi[:, b].bitcast(F32),
                          ALU.subtract).then_inc(self.w_ready[b], 1)

    def multiply(self, pe, turn, b):
        pe.wait_ge(self.w_ready[b], turn + 1)
        for m in range(2):
            for c in range(NC):
                i = m * NC + c
                out, cols, ws = self.banks[i][:, :], slice(c * CW, (c + 1) * CW), slice(m * P, (m + 1) * P)
                pe.wait_ge(self.free[i], 2 * turn + b + 1)
                for k in range(KT):
                    hi, lo = self.w_hi[:, b, k, ws], self.w_lo[:, b, k, ws]
                    pe.matmul(out, hi, self.act_hi[:, k, cols], start=(k == 0), stop=False)
                    pe.matmul(out, hi, self.act_lo[:, k, cols], start=False, stop=False)
                    mm = pe.matmul(out, lo, self.act_hi[:, k, cols], start=False, stop=(k == KT - 1))
                mm.then_inc(self.full[b][i], 1)


def make_identity(pool, ident, zeroed, done):
    pool.memset(ident[:, :], 0.0).then_inc(zeroed, 1)
    pool.wait_ge(zeroed, 1)
    pool.affine_select(out=ident[:, :], in_=ident[:, :], compare_op=ALU.not_equal, fill=1.0, base=0,
                       pattern=[[-1, P]], channel_multiplier=1).then_inc(done, 1)


def norm_and_project(nc, x, norm_in, w_in, s):
    x_t = x.rearrange("a (t p) d -> (a t) p d", p=P)
    w_k = w_in.rearrange("a (k p) f -> p (a k) f", p=P)
    U, VA, ZA, Q, K, VB, ZB, GA, GB = (i * D for i in range(9))
    single = [(VA, ACT.Gelu_apprx_tanh, s["va_T"]), (Q, ACT.Copy, s["q_T"]), (K, ACT.Copy, s["k_T"]),
              (VB, ACT.Copy, s["vb_T"]), (ZB, ACT.Silu, s["zb_T"]), (GA, ACT.Sigmoid, s["ga_T"]),
              (GB, ACT.Sigmoid, s["gb_T"])]
    UZ = KT // 2
    PER = D // WT // 2
    TURNS = UZ + PER * len(single)

    with ExitStack() as memory:
        sc = Scope(nc, memory, "in")
        h_hi = sc.sb("h_hi", [P, KT, S], F32R)
        h_lo = sc.sb("h_lo", [P, KT, S], F32R)
        banks = [sc.ps(f"bank{i}", [P, CW]) for i in range(BANKS)]
        pj = Projection(sc, h_hi, h_lo, banks)
        o_sb = sc.sb("o_sb", [P, BANKS, CW])
        x_sb = sc.sb("x_sb", [P, 2, D])
        gain = sc.sb("gain", [P, D])
        ident = sc.sb("ident", [P, P])
        sq_sum = sc.sb("sq_sum", [P, 2])
        mean_sq = sc.sb("mean_sq", [P, 2])
        inv_rms = sc.sb("inv_rms", [P, 2])
        minus_half = sc.sb("minus_half", [P, 1])

        gain_loaded, zeroed, ident_done, half_set = (
            sc.sem(n) for n in ("gain_loaded", "zeroed", "ident_done", "half_set"))
        x_loaded = sc.sems("x_loaded", 2)
        squared = sc.sems("squared", 2)
        mean_done = sc.sems("mean_done", 2)
        rms_done = sc.sems("rms_done", 2)
        scaled = sc.sems("scaled", 2)
        turned = sc.sems("turned", 2)
        hi_done = sc.sems("hi_done", 2)
        lo_done = sc.sems("lo_done", 2)
        multiplied = sc.sems("multiplied", NC)
        stored = sc.sems("stored", BANKS)
        memory.callback(sc.clear)
        block = memory.enter_context(nc.Block())

        @block.sync
        def _(sp):
            sp.dma_start(x_sb[:, 0], x_t[0]).then_inc(x_loaded[0], 16)
            sp.dma_start(x_sb[:, 1], x_t[1]).then_inc(x_loaded[1], 16)
            sp.dma_start(gain[:, :], norm_in[0:1, :].to_broadcast([P, D])).then_inc(gain_loaded, 16)
            for b in range(2):
                pj.load(sp, 0, b, [(pj.stage[:, b, :, 0:P], w_k[:, :, b * P:(b + 1) * P]),
                                   (pj.stage[:, b, :, P:WT], w_k[:, :, ZA + b * P:ZA + (b + 1) * P])])
            with sp.Fori(1, NT // 2) as t:
                for b in range(2):
                    tile = sp.snap(2 * t + b)
                    sp.wait_ge(turned[b], t)
                    sp.dma_start(x_sb[:, b], x_t[bass.ds(tile, 1)].rearrange("a p d -> p (a d)"))\
                        .then_inc(x_loaded[b], 16)
            with sp.Fori(1, UZ) as t:
                for b in range(2):
                    u_at, z_at = sp.snap(U + (2 * t + b) * P), sp.snap(ZA + (2 * t + b) * P)
                    pj.load(sp, t, b, [(pj.stage[:, b, :, 0:P], w_k[:, :, bass.ds(u_at, P)]),
                                       (pj.stage[:, b, :, P:WT], w_k[:, :, bass.ds(z_at, P)])])
            for n, (at, _, _) in enumerate(single):
                with sp.Fori(0, PER) as t:
                    for b in range(2):
                        w_at = sp.snap(at + (2 * t + b) * WT)
                        pj.load(sp, t + (UZ + n * PER), b, pj.by_rows(b, w_k, w_at))

        @block.gpsimd
        def _(pool):
            pool.memset(minus_half[:, :], -0.5).then_inc(half_set, 1)
            make_identity(pool, ident, zeroed, ident_done)
            pool.wait_ge(half_set, 1)
            with pool.Fori(0, NT // 2) as t:
                for b in range(2):
                    pool.wait_ge(mean_done[b], t + 1)
                    pool.tensor_tensor(inv_rms[:, b:b + 1], mean_sq[:, b:b + 1], minus_half[:, :],
                                       ALU.pow).then_inc(rms_done[b], 1)
            with pool.Fori(0, UZ) as t:
                for b in range(2):
                    for c in range(NC):
                        pool.wait_ge(pj.free[c], 2 * t + b + 2)
                        pool.wait_ge(pj.free[NC + c], 2 * t + b + 2)
                        pool.tensor_tensor(o_sb[:, c], o_sb[:, c], o_sb[:, NC + c], ALU.mult)\
                            .then_inc(multiplied[c], 1)

        @block.scalar
        def _(act):
            def sum_squares(t, b):
                act.wait_ge(x_loaded[b], 16 * t + 16)
                act.activation(o_sb[:, 2 * b:2 * b + 2].rearrange("p a c -> p (a c)"), x_sb[:, b], ACT.Square,
                               accum_out=sq_sum[:, b:b + 1]).then_inc(squared[b], 1)

            def round_hi(t, b, at):
                act.wait_ge(turned[b], t + 1)
                for half in range(2):
                    ins = act.activation(h_hi[:, 4 * half:4 * half + 4, bass.ds(at, P)],
                                         banks[2 * b + half][:, :].rearrange("p (k c) -> p k c", k=4), ACT.Copy)
                ins.then_inc(hi_done[b], 1)

            sum_squares(0, 0)
            with act.Fori(0, NT // 2 - 1) as t:
                sum_squares(t, 1)
                round_hi(t, 0, 2 * t * P)
                sum_squares(t + 1, 0)
                round_hi(t, 1, (2 * t + 1) * P)
            last = NT // 2 - 1
            sum_squares(last, 1)
            round_hi(last, 0, 2 * last * P)
            round_hi(last, 1, (2 * last + 1) * P)

            act.wait_ge(squared[1], NT // 2)

            pj.start(act)

            def gelu_silu(t):
                for b in range(2):
                    row = (2 * t + b) * P
                    for c in range(NC):
                        act.wait_ge(pj.full[b][c], t + 1)
                        wait_past(act, stored[c], 16 * (2 * t + b))
                        act.activation(o_sb[:, c], banks[c][:, :], ACT.Gelu_apprx_tanh).then_inc(pj.free[c], 1)
                    for c in range(NC):
                        i = NC + c
                        act.wait_ge(pj.full[b][i], t + 1)
                        wait_past(act, multiplied[c], 2 * t + b)
                        act.activation(o_sb[:, i], banks[i][:, :], ACT.Silu).then_inc(pj.free[i], 1)
                    for c in range(NC):
                        act.wait_ge(multiplied[c], 2 * t + b + 1)
                        act.dma_start(s["uz_T"][bass.ds(row, P), c * CW:(c + 1) * CW], o_sb[:, c])\
                            .then_inc(stored[c], 16)

            turns_from_first(act, UZ, gelu_silu)
            for n, (_, func, dst) in enumerate(single):
                before = UZ + n * PER

                def one_output(t):
                    for b in range(2):
                        for i in range(BANKS):
                            m, c = divmod(i, NC)
                            row = ((2 * t + b) * 2 + m) * P
                            step = 2 * (t + before) + b
                            act.wait_ge(pj.full[b][i], t + (before + 1))
                            wait_past(act, stored[i], 16 * (step - (0 if i < NC else 2 * UZ)))
                            act.activation(o_sb[:, i], banks[i][:, :], func).then_inc(pj.free[i], 1)
                            act.wait_ge(pj.free[i], step + 2)
                            act.dma_start(dst[bass.ds(row, P), c * CW:(c + 1) * CW], o_sb[:, i])\
                                .then_inc(stored[i], 16)

                if n == 0:
                    turns_from_first(act, PER, one_output)
                else:
                    with act.Fori(0, PER) as t:
                        one_output(t)
            for i in range(BANKS):
                act.wait_ge(stored[i], 16 * 2 * (TURNS if i < NC else TURNS - UZ))

        @block.vector
        def _(dve):
            def mean(t, b):
                dve.wait_ge(squared[b], t + 1)
                dve.tensor_scalar(mean_sq[:, b:b + 1], sq_sum[:, b:b + 1], 1.0 / D, EPS, ALU.mult, ALU.add)\
                    .then_inc(mean_done[b], 1)

            def scale(t, b):
                dve.wait_ge(rms_done[b], t + 1)
                dve.scalar_tensor_tensor(x_sb[:, b], x_sb[:, b], inv_rms[:, b:b + 1], gain[:, :], ALU.mult,
                                         ALU.mult).then_inc(scaled[b], 1)

            def rest_lo(t, b, at):
                dve.wait_ge(hi_done[b], t + 1)
                for half in range(2):
                    ks = slice(4 * half, 4 * half + 4)
                    ins = dve.tensor_tensor(h_lo[:, ks, bass.ds(at, P)],
                                            banks[2 * b + half][:, :].rearrange("p (k c) -> p k c", k=4),
                                            h_hi[:, ks, bass.ds(at, P)].bitcast(F32), ALU.subtract)
                ins.then_inc(lo_done[b], 1)

            for b in range(2):
                dve.sem_inc(lo_done[b], 1)
            dve.wait_ge(gain_loaded, 16)
            mean(0, 0)
            scale(0, 0)
            with dve.Fori(0, NT // 2 - 1) as t:
                mean(t, 1)
                scale(t, 1)
                rest_lo(t, 0, 2 * t * P)
                mean(t + 1, 0)
                scale(t + 1, 0)
                rest_lo(t, 1, (2 * t + 1) * P)
            last = NT // 2 - 1
            mean(last, 1)
            scale(last, 1)
            rest_lo(last, 0, 2 * last * P)
            rest_lo(last, 1, (2 * last + 1) * P)

            def split(t):
                for b in range(2):
                    pj.split(dve, t, b)

            turns_from_first(dve, TURNS, split)

        @block.tensor
        def _(pe):
            pe.wait_ge(ident_done, 1)
            with pe.Fori(0, NT // 2) as t:
                for b in range(2):
                    pe.wait_ge(scaled[b], t + 1)
                    pe.wait_ge(lo_done[b], t + 1)
                    for k in range(KT):
                        ins = pe.transpose(banks[2 * b + k // 4][:, (k % 4) * P:(k % 4 + 1) * P],
                                           x_sb[:, b, k * P:(k + 1) * P], ident[:, :])
                    ins.then_inc(turned[b], 1)
            for b in range(2):
                pe.wait_ge(lo_done[b], NT // 2 + 1)
            with pe.Fori(0, TURNS) as t:
                for b in range(2):
                    pj.multiply(pe, t, b)


def spatial_gating(nc, norm_v, w_s, b_s, s):
    va_n = s["va_T"].rearrange("(g c) s -> c g s", c=P)
    uz_n = s["uz_T"].rearrange("(g c) s -> c g s", c=P)
    ya_n = s["ya_T"].rearrange("(g c) s -> c g s", c=P)
    with ExitStack() as memory:
        sc = Scope(nc, memory, "mix")
        ident = sc.sb("ident", [P, P])
        w_sb = sc.sb("w_sb", [P, GROUPS, P])
        wT_hi = sc.sb("wT_hi", [P, GROUPS, P], F32R)
        wT_lo = sc.sb("wT_lo", [P, GROUPS, P], F32R)
        bias = sc.sb("bias", [P, GROUPS, P])
        gain = sc.sb("gain", [P, GROUPS])
        va = sc.sb("va", [P, 2, GROUPS, P])
        uz = sc.sb("uz", [P, 2, GROUPS, P])
        v_hi = sc.sb("v_hi", [P, 2, D], F32R)
        v_lo = sc.sb("v_lo", [P, 2, D], F32R)
        y = sc.sb("y", [P, 2, GROUPS, P])
        squares = sc.sb("squares", [P, D])
        sq_sum, mean_sq, inv_rms = (sc.sb(n, [P, 2]) for n in ("sq_sum", "mean_sq", "inv_rms"))
        minus_half = sc.sb("minus_half", [P, 1])
        v_ps = [sc.ps(f"v_ps{b}", [P, D]) for b in range(2)]
        m_ps = [sc.ps(f"m_ps{b}", [P, D]) for b in range(2)]

        w_loaded, bias_loaded, gain_loaded, zeroed, ident_done, half_set, masked, w_turned, w_hi_done, w_done = (
            sc.sem(n) for n in ("w_loaded", "bias_loaded", "gain_loaded", "zeroed", "ident_done", "half_set",
                                "masked", "w_turned", "w_hi_done", "w_done"))
        va_loaded, uz_loaded, turned, squared, mean_done, rms_done, hi_done, lo_done, mixed, gained, biased, y_done, \
            stored = (sc.sems(n, 2) for n in (
                "va_loaded", "uz_loaded", "turned", "squared", "mean_done", "rms_done", "hi_done", "lo_done",
                "mixed", "gained", "biased", "y_done", "stored"))
        memory.callback(sc.clear)
        block = memory.enter_context(nc.Block())

        @block.sync
        def _(sp):
            sp.dma_start(w_sb[:, :, :], w_s[0].rearrange("g t s -> t g s")).then_inc(w_loaded, 16)
            sp.dma_start(bias[:, :, :].rearrange("p g t -> p (g t)"),
                         b_s.rearrange("a g t -> a (g t)").to_broadcast([P, D])).then_inc(bias_loaded, 16)
            with nc.allow_non_contiguous_dma(reason="1024 gains, one to a partition"):
                sp.dma_start(gain[:, :], norm_v[0].rearrange("(g c) -> c g", c=P)).then_inc(gain_loaded, 16)

            def load(t):
                for b in range(2):
                    at = (2 * t + b) * P if isinstance(t, int) else sp.snap((2 * t + b) * P)
                    wait_past(sp, turned[b], t)
                    sp.dma_start(va[:, b], va_n[:, :, bass.ds(at, P)]).then_inc(va_loaded[b], 16)
                    wait_past(sp, y_done[b], t)
                    sp.dma_start(uz[:, b], uz_n[:, :, bass.ds(at, P)]).then_inc(uz_loaded[b], 16)

            turns_from_first(sp, NT // 2, load)

        @block.gpsimd
        def _(pool):
            pool.memset(minus_half[:, :], -0.5).then_inc(half_set, 1)
            make_identity(pool, ident, zeroed, ident_done)
            pool.wait_ge(w_loaded, 16)
            pool.affine_select(out=w_sb[:, :, :], in_=w_sb[:, :, :], compare_op=ALU.is_ge, fill=0.0, base=0,
                               pattern=[[0, GROUPS], [-1, P]], channel_multiplier=1).then_inc(masked, 1)
            pool.wait_ge(half_set, 1)
            pool.wait_ge(bias_loaded, 16)
            with pool.Fori(0, NT // 2) as t:
                for b in range(2):
                    pool.wait_ge(mean_done[b], t + 1)
                    pool.tensor_tensor(inv_rms[:, b:b + 1], mean_sq[:, b:b + 1], minus_half[:, :],
                                       ALU.pow).then_inc(rms_done[b], 1)
                for b in range(2):
                    pool.wait_ge(gained[b], t + 1)
                    pool.tensor_tensor(y[:, b], y[:, b], bias[:, :, :], ALU.add).then_inc(biased[b], 1)

        @block.scalar
        def _(act):
            act.wait_ge(w_turned, 1)
            act.activation(wT_hi[:, :, :].rearrange("p g t -> p (g t)"), m_ps[0][:, :], ACT.Copy).then_inc(w_hi_done, 1)

            def store(t, b, at):
                act.wait_ge(y_done[b], t + 1)
                act.dma_start(ya_n[:, :, bass.ds(at, P)], y[:, b]).then_inc(stored[b], 16)

            def normalise(t):
                for b in range(2):
                    act.wait_ge(turned[b], t + 1)
                    act.activation(squares[:, :], v_ps[b][:, :], ACT.Square,
                                   accum_out=sq_sum[:, b:b + 1]).then_inc(squared[b], 1)
                    act.wait_ge(rms_done[b], t + 1)
                    wait_past(act, mixed[b], t)
                    act.activation(v_hi[:, b], v_ps[b][:, :], ACT.Copy, scale=inv_rms[:, b:b + 1])\
                        .then_inc(hi_done[b], 1)
                for b in range(2):
                    store(t, b, (2 * t + b) * P)

            turns_from_first(act, NT // 2, normalise)
            for b in range(2):
                act.wait_ge(stored[b], 16 * (NT // 2))

        @block.vector
        def _(dve):
            dve.wait_ge(w_hi_done, 1)
            dve.tensor_tensor(wT_lo[:, :, :].rearrange("p g t -> p (g t)"), m_ps[0][:, :],
                              wT_hi[:, :, :].rearrange("p g t -> p (g t)").bitcast(F32), ALU.subtract)\
                .then_inc(w_done, 1)
            dve.wait_ge(gain_loaded, 16)

            def gate(t):
                for b in range(2):
                    dve.wait_ge(squared[b], t + 1)
                    dve.tensor_scalar(mean_sq[:, b:b + 1], sq_sum[:, b:b + 1], 1.0 / D, EPS, ALU.mult,
                                      ALU.add).then_inc(mean_done[b], 1)
                    dve.wait_ge(hi_done[b], t + 1)
                    dve.scalar_tensor_tensor(v_lo[:, b], v_ps[b][:, :], inv_rms[:, b:b + 1],
                                             v_hi[:, b].bitcast(F32), ALU.mult, ALU.subtract)\
                        .then_inc(lo_done[b], 1)
                for b in range(2):
                    dve.wait_ge(mixed[b], t + 1)
                    wait_past(dve, stored[b], 16 * t)
                    dve.tensor_tensor(y[:, b], m_ps[b][:, :].rearrange("p (g t) -> p g t", g=GROUPS),
                                      gain[:, :].unsqueeze(2).to_broadcast([P, GROUPS, P]), ALU.mult)\
                        .then_inc(gained[b], 1)
                    dve.wait_ge(biased[b], t + 1)
                    dve.wait_ge(uz_loaded[b], 16 * t + 16)
                    dve.tensor_tensor(y[:, b], y[:, b], uz[:, b], ALU.mult).then_inc(y_done[b], 1)

            turns_from_first(dve, NT // 2, gate)

        @block.tensor
        def _(pe):
            pe.wait_ge(ident_done, 1)
            pe.wait_ge(masked, 1)
            for g in range(GROUPS):
                ins = pe.transpose(m_ps[0][:, g * P:(g + 1) * P], w_sb[:, g, :], ident[:, :])
            ins.then_inc(w_turned, 1)
            pe.wait_ge(w_done, 1)

            def mix(t):
                for b in range(2):
                    pe.wait_ge(va_loaded[b], 16 * t + 16)
                    wait_past(pe, lo_done[b], t)
                    for g in range(GROUPS):
                        ins = pe.transpose(v_ps[b][:, g * P:(g + 1) * P], va[:, b, g, :], ident[:, :])
                    ins.then_inc(turned[b], 1)
                for b in range(2):
                    pe.wait_ge(lo_done[b], t + 1)
                    wait_past(pe, gained[b], t)
                    for g in range(GROUPS):
                        gs = slice(g * P, (g + 1) * P)
                        pe.matmul(m_ps[b][:, gs], v_hi[:, b, gs], wT_hi[:, g], start=True, stop=False)
                        pe.matmul(m_ps[b][:, gs], v_hi[:, b, gs], wT_lo[:, g], start=False, stop=False)
                        mm = pe.matmul(m_ps[b][:, gs], v_lo[:, b, gs], wT_hi[:, g], start=False, stop=True)
                    mm.then_inc(mixed[b], 1)

            turns_from_first(pe, NT // 2, mix)


def blend(some, others):
    at = [((n + 0.5) / len(some), 0, e) for n, e in enumerate(some)]
    at += [((n + 0.5) / len(others), 1, e) for n, e in enumerate(others)]
    return [e for _, _, e in sorted(at, key=lambda a: a[:2])]


QT = CW // P
NSUP = NT // QT
ZW = 1024


def z_pieces(sup):
    return [("Z", i, at, min(ZW, (i + 1) * P - at)) for i in range(sup * QT, (sup + 1) * QT)
            for at in range(0, (i + 1) * P, ZW)]


def turns_of(sup):
    return [("B", sup, kt) for kt in range((sup + 1) * QT)]


def head_order(last):
    def with_y(blended, sup):
        at = [n for n, e in enumerate(blended) if e[0] == "B"][1] + 1
        return blended[:at] + [("Y", sup)] + blended[at:]

    order = blend(z_pieces(1), [("V", g) for g in range(NT // QT)] + turns_of(0))
    order += with_y(blend(z_pieces(2), turns_of(1)), 0)
    order += with_y(blend(z_pieces(3), turns_of(2)), 1)
    if last:
        order += with_y(turns_of(3), 2)
    else:
        order += [("QK",)] + with_y(blend(z_pieces(0), turns_of(3)), 2)
    return order + [("Y", 3)]


def attention(nc, s):
    PIECES = sum(len(z_pieces(n)) for n in range(NSUP))
    PRODUCTS = sum(len(turns_of(n)) for n in range(NSUP))
    STEPS = NT // QT + PRODUCTS
    SLOTS = 2 * QT
    FIRST = len(z_pieces(0))
    assert PIECES % 2 == 0 and STEPS % 2 == 0 and PRODUCTS % 2 == 0

    with ExitStack() as memory:
        sc = Scope(nc, memory, "att")
        ident = sc.sb("ident", [P, P])
        ident_r = sc.sb("ident_r", [P, P], F32R)
        mask = sc.sb("mask", [P, P])
        mask_r = sc.sb("mask_r", [P, P], F32R)
        q_in, k_in, v_in = (sc.sb(n, [P, S]) for n in ("q_in", "k_in", "v_in"))
        q_hi, q_lo, k_hi, k_lo = (sc.sb(n, [P, S], F32R) for n in ("q_hi", "q_lo", "k_hi", "k_lo"))
        v_hi, v_lo = (sc.sb(n, [P, S], F32R) for n in ("v_hi", "v_lo"))
        slot = [sc.sb(f"slot{n}", [P, (n + 1 + SLOTS) * P]) for n in range(SLOTS)]
        rest = [sc.sb(f"rest{n}", [P, S + 1]) for n in range(2)]
        wT_hi = [sc.sb(f"wT_hi{n}", [P, CW], F32R) for n in range(2)]
        wT_lo = [sc.sb(f"wT_lo{n}", [P, CW], F32R) for n in range(2)]
        zb = [sc.sb(f"zb{n}", [P, CW]) for n in range(2)]
        y = [sc.sb(f"y{n}", [P, CW]) for n in range(2)]
        z_ps = [sc.ps(f"z_ps{n}", [P, ZW]) for n in range(2)]
        t_ps = [sc.ps(f"t_ps{n}", [P, CW]) for n in range(2)]
        y_ps = [sc.ps(f"y_ps{n}", [P, CW]) for n in range(2)]

        zeroed, ident_done, mask_zeroed, mask_done, consts, ones_set = (
            sc.sem(n) for n in ("zeroed", "ident_done", "mask_zeroed", "mask_done", "consts", "ones_set"))
        qk_loaded, v_loaded = sc.sem("qk_loaded"), sc.sem("v_loaded")
        qk_hi, qk_done = sc.sem("qk_hi"), sc.sem("qk_done")
        z_full = sc.sem("z_full")
        z_read = sc.sems("z_read", 2)
        scanned = sc.sem("scanned")
        weighted = sc.sem("weighted")
        turned = sc.sem("turned")
        hi_done = sc.sem("hi_done")
        lo_done = sc.sems("lo_done", 2)
        product = sc.sems("product", 2)
        zb_loaded, y_done, stored = (sc.sems(n, 2) for n in ("zb_loaded", "y_done", "stored"))
        memory.callback(sc.clear)
        block = memory.enter_context(nc.Block())

        def position(order):
            seen, out = {"Z": 0, "T": 0, "B": 0}, []
            for e in order:
                out.append(dict(seen))
                if e[0] == "Z":
                    seen["Z"] += 1
                if e[0] in "VB":
                    seen["T"] += 1
                if e[0] == "B":
                    seen["B"] += 1
            return out

        def steps_until(order, sup):
            return max(p["T"] + 1 for e, p in zip(order, position(order)) if e[:2] == ("B", sup))

        V_READ = max(p["T"] + 1 for e, p in zip(head_order(False), position(head_order(False))) if e[0] == "V")

        def products_until(sup):
            return sum(len(turns_of(n)) for n in range(sup + 1))

        def per_head(eng, body):
            body(0, False)
            with eng.Fori(1, HEADS - 1) as h:
                body(h, False)
            body(HEADS - 1, True)

        @block.sync
        def _(sp):
            def load_qk(h):
                row = h * P if isinstance(h, int) else sp.snap(h * P)
                if not isinstance(h, int) or h > 0:
                    sp.wait_ge(qk_done, h)
                sp.dma_start(q_in[:, :], s["q_T"][bass.ds(row, P), :]).then_inc(qk_loaded, 16)
                sp.dma_start(k_in[:, :], s["k_T"][bass.ds(row, P), :]).then_inc(qk_loaded, 16)

            def body(h, last):
                row = h * P if isinstance(h, int) else sp.snap(h * P)
                nxt = (h + 1) * P if isinstance(h, int) else sp.snap((h + 1) * P)
                if not last:
                    load_qk(h + 1)
                for sup in range(NSUP):
                    n = sup % 2
                    cols = slice(sup * CW, (sup + 1) * CW)
                    if sup >= 1:
                        m = (sup - 1) % 2
                        sp.wait_ge(y_done[m], 2 * h + ((sup - 1) // 2 + 1))
                        sp.dma_start(s["yb_T"][bass.ds(row, P), (sup - 1) * CW:sup * CW], y[m][:, :])\
                            .then_inc(stored[m], 16)
                    wait_past(sp, y_done[n], 2 * h + sup // 2)
                    sp.dma_start(zb[n][:, :], s["zb_T"][bass.ds(row, P), cols]).then_inc(zb_loaded[n], 16)
                    if sup == 0 and not last:
                        sp.wait_ge(turned, STEPS * h + V_READ)
                        sp.dma_start(v_in[:, :], s["vb_T"][bass.ds(nxt, P), :]).then_inc(v_loaded, 16)
                sp.wait_ge(y_done[1], 2 * h + 2)
                sp.dma_start(s["yb_T"][bass.ds(row, P), (NSUP - 1) * CW:], y[1][:, :]).then_inc(stored[1], 16)

            load_qk(0)
            sp.dma_start(v_in[:, :], s["vb_T"][0:P, :]).then_inc(v_loaded, 16)
            per_head(sp, body)
            for n in range(2):
                sp.wait_ge(stored[n], 16 * 2 * HEADS)

        @block.gpsimd
        def _(pool):
            make_identity(pool, ident, zeroed, ident_done)
            pool.memset(mask[:, :], 0.0).then_inc(mask_zeroed, 1)
            pool.wait_ge(mask_zeroed, 1)
            pool.affine_select(out=mask[:, :], in_=mask[:, :], compare_op=ALU.is_gt, fill=MASKED, base=0,
                               pattern=[[-1, P]], channel_multiplier=1).then_inc(mask_done, 1)

        @block.scalar
        def _(act):
            def split_qk(h):
                act.wait_ge(qk_loaded, 32 * h + 32)
                wait_past(act, z_full, PIECES * h)
                act.activation(q_hi[:, :], q_in[:, :], ACT.Copy)
                act.activation(k_hi[:, :], k_in[:, :], ACT.Copy).then_inc(qk_hi, 1)

            def sigmoids(i, at, width, piece, tile, slot_free):
                par = piece % 2 if isinstance(piece, int) else piece[1]
                count = piece if isinstance(piece, int) else piece[0]
                src = z_ps[par][:, 0:width]
                right = S - (i + 1) * P + at
                act.wait_ge(z_full, count + 1)
                if slot_free is not None and at == 0:
                    wait_past(act, turned, slot_free)
                act.activation(slot[i % SLOTS][:, at:at + width], src, ACT.Sigmoid, scale=SCALE)
                if tile is not None and at == 0:
                    act.wait_ge(weighted, tile)
                act.activation(rest[i % 2][:, right:right + width], src, ACT.Sigmoid, scale=-SCALE)\
                    .then_inc(z_read[par], 1)

            def body(h, last):
                order = head_order(last)
                for e, p in zip(order, position(order)):
                    if e[0] == "Z":
                        _, i, at, width = e
                        sup = i // QT
                        count = PIECES * h + (FIRST + p["Z"])
                        tiles = NT * h + (i - 1 if sup else NT + i - 1)
                        free = {0: STEPS * h + steps_until(order, 2), 1: STEPS * h,
                                2: STEPS * h + steps_until(order, 0), 3: STEPS * h + steps_until(order, 1)}[sup]
                        sigmoids(i, at, width, (count, (FIRST + p["Z"]) % 2), tiles, free)
                    elif e[0] == "QK":
                        split_qk(h + 1)
                    elif e[0] in "VB":
                        t = p["T"]
                        act.wait_ge(turned, STEPS * h + (t + 1))
                        if e[0] == "V":
                            if e[1] == 0:
                                for n in range(2):
                                    wait_past(act, product[n], PRODUCTS // 2 * h)
                            act.activation(v_hi[:, e[1] * CW:(e[1] + 1) * CW], t_ps[t % 2][:, :], ACT.Copy)\
                                .then_inc(hi_done, 1)
                        else:
                            n, c0 = p["B"] % 2, max(0, e[2] - QT * e[1]) * P
                            wait_past(act, product[n], PRODUCTS // 2 * h + p["B"] // 2)
                            act.activation(wT_hi[n][:, c0:], t_ps[t % 2][:, c0:], ACT.Copy).then_inc(hi_done, 1)

            split_qk(0)
            act.wait_ge(ones_set, 2)
            for n, (_, i, at, width) in enumerate(z_pieces(0)):
                sigmoids(i, at, width, n, i - 1 if i >= 2 else None, None)
            per_head(act, body)

        @block.vector
        def _(dve):
            def split_qk(h):
                dve.wait_ge(qk_hi, h + 1)
                dve.tensor_tensor(q_lo[:, :], q_in[:, :], q_hi[:, :].bitcast(F32), ALU.subtract)
                dve.tensor_tensor(k_lo[:, :], k_in[:, :], k_hi[:, :].bitcast(F32), ALU.subtract)\
                    .then_inc(qk_done, 1)

            def weights(i, at, width, reads, tile):
                if at + width < (i + 1) * P:
                    return
                for n, count in reads:
                    dve.wait_ge(z_read[n], count)
                w = (i + 1) * P
                r = rest[i % 2]
                dve.tensor_tensor_scan(out=r[:, S - w:S][:, ::-1], data0=r[:, S - w:S][:, ::-1],
                                       data1=r[:, S - w:S][:, ::-1], initial=r[:, S:S + 1], op0=ALU.mult,
                                       op1=ALU.bypass).then_inc(scanned, 1)
                dve.wait_ge(scanned, tile + 1)
                a = slot[i % SLOTS]
                dve.tensor_tensor(a[:, 0:w], a[:, 0:w], r[:, S - w + 1:S + 1], ALU.mult).then_inc(weighted, 1)

            def body(h, last):
                order = head_order(last)
                for e, p in zip(order, position(order)):
                    if e[0] == "Z":
                        _, i, at, width = e
                        n = FIRST + p["Z"]
                        reads = [(n % 2, PIECES // 2 * h + (n // 2 + 1))]
                        weights(i, at, width, reads, NT * h + (i if i >= QT else NT + i))
                    elif e[0] == "QK":
                        split_qk(h + 1)
                    elif e[0] in "VB":
                        t = p["T"]
                        dve.wait_ge(hi_done, STEPS * h + (t + 1))
                        if e[0] == "V":
                            cols = slice(e[1] * CW, (e[1] + 1) * CW)
                            dve.tensor_tensor(v_lo[:, cols], t_ps[t % 2][:, :], v_hi[:, cols].bitcast(F32),
                                              ALU.subtract).then_inc(lo_done[t % 2], 1)
                        else:
                            n, c0 = p["B"] % 2, max(0, e[2] - QT * e[1]) * P
                            dve.tensor_tensor(wT_lo[n][:, c0:], t_ps[t % 2][:, c0:],
                                              wT_hi[n][:, c0:].bitcast(F32), ALU.subtract)\
                                .then_inc(lo_done[t % 2], 1)
                    elif e[0] == "Y":
                        sup, n = e[1], e[1] % 2
                        done = products_until(sup)
                        dve.wait_ge(product[(done - 1) % 2], PRODUCTS // 2 * h + (done + 1) // 2)
                        dve.wait_ge(zb_loaded[n], 32 * h + 16 * (sup // 2 + 1))
                        wait_past(dve, stored[n], 32 * h + 16 * (sup // 2))
                        dve.tensor_tensor(y[n][:, :], y_ps[n][:, :], zb[n][:, :], ALU.mult).then_inc(y_done[n], 1)

            dve.memset(rest[0][:, S:S + 1], 1.0).then_inc(ones_set, 1)
            dve.memset(rest[1][:, S:S + 1], 1.0).then_inc(ones_set, 1)
            dve.wait_ge(ident_done, 1)
            dve.tensor_copy(ident_r[:, :], ident[:, :]).then_inc(consts, 1)
            dve.wait_ge(mask_done, 1)
            dve.tensor_copy(mask_r[:, :], mask[:, :]).then_inc(consts, 1)
            split_qk(0)
            for n, (_, i, at, width) in enumerate(z_pieces(0)):
                weights(i, at, width, [(n % 2, n // 2 + 1)], i)
            per_head(dve, body)

        @block.tensor
        def _(pe):
            def logits(i, at, width, par, reads):
                if reads is not None:
                    pe.wait_ge(z_read[par], reads)
                qs = slice(i * P, (i + 1) * P)
                for c in range(0, width, CW):
                    w = min(CW, width - c)
                    out = z_ps[par][:, c:c + w]
                    ks = slice(at + c, at + c + w)
                    diagonal = at + c + w == (i + 1) * P
                    pe.matmul(out, q_hi[:, qs], k_hi[:, ks], start=True, stop=False)
                    pe.matmul(out, q_hi[:, qs], k_lo[:, ks], start=False, stop=False)
                    mm = pe.matmul(out, q_lo[:, qs], k_hi[:, ks], start=False, stop=not diagonal)
                    if diagonal:
                        mm = pe.matmul(z_ps[par][:, c + w - P:c + w], ident_r[:, :], mask_r[:, :],
                                       start=False, stop=True)
                mm.then_inc(z_full, 1)

            def multiply(h, order, pos, n):
                k = [j for j, e in enumerate(order) if e[0] == "B"][n]
                _, sup, kt = order[k]
                t, c0, par = pos[k]["T"], max(0, kt - QT * sup) * P, n % 2
                pe.wait_ge(lo_done[t % 2], STEPS // 2 * h + (t // 2 + 1))
                if kt == 0:
                    wait_past(pe, y_done[sup % 2], 2 * h + sup // 2)
                vs, out = slice(kt * P, (kt + 1) * P), y_ps[sup % 2][:, c0:]
                end = kt == (sup + 1) * QT - 1
                pe.matmul(out, v_hi[:, vs], wT_hi[par][:, c0:], start=(kt == 0), stop=False)
                pe.matmul(out, v_hi[:, vs], wT_lo[par][:, c0:], start=False, stop=False)
                pe.matmul(out, v_lo[:, vs], wT_hi[par][:, c0:], start=False, stop=end).then_inc(product[par], 1)

            def body(h, last):
                order = head_order(last)
                pos = position(order)
                for e, p in zip(order, pos):
                    if e[0] == "Z":
                        _, i, at, width = e
                        n = FIRST + p["Z"]
                        logits(i, at, width, n % 2, PIECES // 2 * h + n // 2)
                    elif e[0] == "QK":
                        pe.wait_ge(qk_done, h + 2)
                    elif e[0] in "VB":
                        t = p["T"]
                        wait_past(pe, lo_done[t % 2], STEPS // 2 * h + t // 2)
                        if e[0] == "V":
                            if e[1] == 0:
                                pe.wait_ge(v_loaded, 16 * h + 16)
                            for j in range(QT):
                                at = (e[1] * QT + j) * P
                                ins = pe.transpose(t_ps[t % 2][:, j * P:(j + 1) * P], v_in[:, at:at + P], ident[:, :])
                            ins.then_inc(turned, 1)
                        else:
                            _, sup, kt = e
                            for j in range(max(0, kt - QT * sup), QT):
                                i = QT * sup + j
                                if kt == 0:
                                    pe.wait_ge(weighted, NT * h + (i + 1))
                                ins = pe.transpose(t_ps[t % 2][:, j * P:(j + 1) * P],
                                                   slot[i % SLOTS][:, kt * P:(kt + 1) * P], ident[:, :])
                            ins.then_inc(turned, 1)
                            if p["B"] >= 1:
                                multiply(h, order, pos, p["B"] - 1)
                multiply(h, order, pos, PRODUCTS - 1)

            pe.wait_ge(consts, 2)
            pe.wait_ge(qk_done, 1)
            for n, (_, i, at, width) in enumerate(z_pieces(0)):
                logits(i, at, width, n % 2, n // 2 if n >= 2 else None)
            per_head(pe, body)


def branch_projection(nc, name, y_T, weights, gate_T, other_T, out_T):
    w_k = weights.rearrange("a (k p) f -> p (a k) f", p=P)
    STEPS = D // WT
    with ExitStack() as memory:
        sc = Scope(nc, memory, f"br_{name}")
        y_hi = sc.sb("y_hi", [P, KT, S], F32R)
        y_lo = sc.sb("y_lo", [P, KT, S], F32R)
        banks = [sc.ps(f"bank{i}", [P, CW]) for i in range(BANKS)]
        pj = Projection(sc, y_hi, y_lo, banks)
        y_in = sc.sb("y_in", [P, NC, CW])
        gate = sc.sb("gate", [P, NC, CW])
        other = sc.sb("other", [P, NC, CW]) if other_T is not None else None
        y_loaded, y_hi_done, y_lo_done, gate_loaded, added, stored = (
            sc.sems(n, NC) for n in ("y_loaded", "y_hi_done", "y_lo_done", "gate_loaded", "added", "stored"))
        memory.callback(sc.clear)
        block = memory.enter_context(nc.Block())
        loads = 32 if other_T is not None else 16

        def tiles():
            return [(it, m, c) for it in range(STEPS) for m in range(2) for c in range(NC)]

        @block.sync
        def _(sp):
            for b in range(2):
                pj.load(sp, 0, b, pj.by_rows(b, w_k, b * WT))
            for k in range(KT):
                for c in range(NC):
                    wait_past(sp, y_lo_done[c], k)
                    sp.dma_start(y_in[:, c], y_T[k * P:(k + 1) * P, c * CW:(c + 1) * CW]).then_inc(y_loaded[c], 16)
            for it, m, c in tiles():
                rows = slice((2 * it + m) * P, (2 * it + m + 1) * P)
                wait_past(sp, stored[c], 16 * (2 * it + m))
                sp.dma_start(gate[:, c], gate_T[rows, c * CW:(c + 1) * CW]).then_inc(gate_loaded[c], 16)
                if other_T is not None:
                    sp.dma_start(other[:, c], other_T[rows, c * CW:(c + 1) * CW]).then_inc(gate_loaded[c], 16)
                if (m, c) == (0, 0) and 1 <= it < STEPS - 1:
                    pj.load(sp, (it + 1) // 2, (it + 1) % 2, pj.by_rows((it + 1) % 2, w_k, (it + 1) * WT))

        @block.scalar
        def _(act):
            for k in range(KT):
                for c in range(NC):
                    act.wait_ge(y_loaded[c], 16 * k + 16)
                    act.activation(y_hi[:, k, c * CW:(c + 1) * CW], y_in[:, c], ACT.Copy).then_inc(y_hi_done[c], 1)
            for it, m, c in tiles():
                rows = slice((2 * it + m) * P, (2 * it + m + 1) * P)
                if other_T is not None:
                    act.wait_ge(added[c], 2 * it + m + 1)
                else:
                    act.wait_ge(pj.free[m * NC + c], it + 2)
                act.dma_start(out_T[rows, c * CW:(c + 1) * CW], gate[:, c]).then_inc(stored[c], 16)
            for c in range(NC):
                act.wait_ge(stored[c], 16 * 2 * STEPS)

        @block.vector
        def _(dve):
            pj.start(dve)
            for b in range(2):
                pj.split(dve, 0, b)
            for k in range(KT):
                for c in range(NC):
                    cols = slice(c * CW, (c + 1) * CW)
                    dve.wait_ge(y_hi_done[c], k + 1)
                    dve.tensor_tensor(y_lo[:, k, cols], y_in[:, c], y_hi[:, k, cols].bitcast(F32),
                                      ALU.subtract).then_inc(y_lo_done[c], 1)
            for it, m, c in tiles():
                if (m, c) == (0, 0) and 1 <= it < STEPS - 1:
                    pj.split(dve, (it + 1) // 2, (it + 1) % 2)
                i = m * NC + c
                dve.wait_ge(gate_loaded[c], loads * (2 * it + m + 1))
                dve.wait_ge(pj.full[it % 2][i], it // 2 + 1)
                dve.tensor_tensor(gate[:, c], banks[i][:, :], gate[:, c], ALU.mult).then_inc(pj.free[i], 1)
                if other_T is not None:
                    dve.wait_ge(pj.free[i], it + 2)
                    dve.tensor_tensor(gate[:, c], gate[:, c], other[:, c], ALU.add).then_inc(added[c], 1)

        @block.tensor
        def _(pe):
            for c in range(NC):
                pe.wait_ge(y_lo_done[c], KT)
            with pe.Fori(0, STEPS // 2) as t:
                for b in range(2):
                    pj.multiply(pe, t, b)


def output_projection(nc, x, w_out, norm_final, out, s):
    x_t = x.rearrange("a (t p) d -> (a t) p d", p=P)
    out_t = out.rearrange("a (t p) d -> (a t) p d", p=P)
    m_k = s["merged_T"].rearrange("(k p) s -> p k s", p=P)
    w_k = w_out.rearrange("a (k p) f -> p (a k) f", p=P)
    HALVES = D // CW
    with ExitStack() as memory:
        sc = Scope(nc, memory, "out")
        w_in = sc.sb("w_in", [P, KT, D])
        w_hi = sc.sb("w_hi", [P, KT, D], F32R)
        w_lo = sc.sb("w_lo", [P, KT, D], F32R)
        m_in = sc.sb("m_in", [P, 2, KT, P])
        m_hi = sc.sb("m_hi", [P, 2, KT, P], F32R)
        m_lo = sc.sb("m_lo", [P, 2, KT, P], F32R)
        x_sb = sc.sb("x_sb", [P, 2, D])
        y_sb = sc.sb("y_sb", [P, 2, D])
        squares = sc.sb("squares", [P, D])
        gain = sc.sb("gain", [P, D])
        sq_sum, mean_sq, inv_rms = (sc.sb(n, [P, 2]) for n in ("sq_sum", "mean_sq", "inv_rms"))
        minus_half = sc.sb("minus_half", [P, 1])
        acc = [sc.ps(f"acc{b}", [P, D]) for b in range(2)]
        gain_loaded, half_set = sc.sem("gain_loaded"), sc.sem("half_set")
        w_loaded = sc.sems("w_loaded", KT)
        w_hi_done, w_lo_done = sc.sem("w_hi_done"), sc.sem("w_lo_done")
        m_loaded, m_hi_done, m_lo_done, x_loaded, full, summed, squared, mean_done, rms_done, y_done, stored = (
            sc.sems(n, 2) for n in ("m_loaded", "m_hi_done", "m_lo_done", "x_loaded", "full", "summed", "squared",
                                    "mean_done", "rms_done", "y_done", "stored"))
        memory.callback(sc.clear)
        block = memory.enter_context(nc.Block())

        @block.sync
        def _(sp):
            for b in range(2):
                sp.dma_start(m_in[:, b], m_k[:, :, b * P:(b + 1) * P]).then_inc(m_loaded[b], 16)
            for k in range(KT):
                sp.dma_start(w_in[:, k], w_k[:, k]).then_inc(w_loaded[k], 16)
            for b in range(2):
                sp.dma_start(x_sb[:, b], x_t[b]).then_inc(x_loaded[b], 16)
            sp.dma_start(gain[:, :], norm_final.unsqueeze(0).to_broadcast([P, D])).then_inc(gain_loaded, 16)
            with sp.Fori(1, NT // 2) as t:
                for b in range(2):
                    tile, at = sp.snap(2 * t + b), sp.snap((2 * t + b) * P)
                    sp.wait_ge(m_lo_done[b], t)
                    sp.dma_start(m_in[:, b], m_k[:, :, bass.ds(at, P)]).then_inc(m_loaded[b], 16)
                    sp.wait_ge(y_done[b], t)
                    sp.dma_start(x_sb[:, b], x_t[bass.ds(tile, 1)].rearrange("a p d -> p (a d)"))\
                        .then_inc(x_loaded[b], 16)

        @block.gpsimd
        def _(pool):
            pool.memset(minus_half[:, :], -0.5).then_inc(half_set, 1)
            pool.wait_ge(half_set, 1)
            with pool.Fori(0, NT // 2) as t:
                for b in range(2):
                    pool.wait_ge(mean_done[b], t + 1)
                    pool.tensor_tensor(inv_rms[:, b:b + 1], mean_sq[:, b:b + 1], minus_half[:, :],
                                       ALU.pow).then_inc(rms_done[b], 1)

        @block.scalar
        def _(act):
            def merged_hi(t, b):
                act.wait_ge(m_loaded[b], 16 * t + 16)
                wait_past(act, full[b], t)
                act.activation(m_hi[:, b], m_in[:, b], ACT.Copy).then_inc(m_hi_done[b], 1)

            def finish(t, b, at):
                act.wait_ge(summed[b], t + 1)
                act.activation(squares[:, :], x_sb[:, b], ACT.Square, accum_out=sq_sum[:, b:b + 1])\
                    .then_inc(squared[b], 1)

            def store(t, b, tile):
                act.wait_ge(y_done[b], t + 1)
                act.dma_start(out_t[bass.ds(tile, 1)].rearrange("a p d -> p (a d)"), y_sb[:, b])\
                    .then_inc(stored[b], 16)

            merged_hi(0, 0)
            merged_hi(0, 1)
            for k in range(KT):
                act.wait_ge(w_loaded[k], 16)
                act.activation(w_hi[:, k], w_in[:, k], ACT.Copy).then_inc(w_hi_done, 1)
            with act.Fori(0, NT // 2 - 1) as t:
                for b in range(2):
                    finish(t, b, None)
                    merged_hi(t + 1, b)
                    store(t, b, 2 * t + b)
            last = NT // 2 - 1
            for b in range(2):
                finish(last, b, None)
                store(last, b, 2 * last + b)
            for b in range(2):
                act.wait_ge(stored[b], 16 * (NT // 2))

        @block.vector
        def _(dve):
            def merged_lo(t, b):
                dve.wait_ge(m_hi_done[b], t + 1)
                dve.tensor_tensor(m_lo[:, b], m_in[:, b], m_hi[:, b].bitcast(F32), ALU.subtract)\
                    .then_inc(m_lo_done[b], 1)

            def finish(t, b):
                dve.wait_ge(x_loaded[b], 16 * t + 16)
                dve.wait_ge(full[b], t + 1)
                dve.tensor_tensor(x_sb[:, b], acc[b][:, :], x_sb[:, b], ALU.add).then_inc(summed[b], 1)
                dve.wait_ge(squared[b], t + 1)
                dve.tensor_scalar(mean_sq[:, b:b + 1], sq_sum[:, b:b + 1], 1.0 / D, EPS, ALU.mult, ALU.add)\
                    .then_inc(mean_done[b], 1)
                dve.wait_ge(rms_done[b], t + 1)
                wait_past(dve, stored[b], 16 * t)
                dve.scalar_tensor_tensor(y_sb[:, b], x_sb[:, b], inv_rms[:, b:b + 1], gain[:, :], ALU.mult,
                                         ALU.mult).then_inc(y_done[b], 1)

            merged_lo(0, 0)
            merged_lo(0, 1)
            for k in range(KT):
                dve.wait_ge(w_hi_done, k + 1)
                dve.tensor_tensor(w_lo[:, k], w_in[:, k], w_hi[:, k].bitcast(F32), ALU.subtract)\
                    .then_inc(w_lo_done, 1)
            dve.wait_ge(gain_loaded, 16)

            def turn(t):
                for b in range(2):
                    finish(t, b)
                    merged_lo(t + 1, b)

            turns_from_first(dve, NT // 2 - 1, turn)
            for b in range(2):
                finish(NT // 2 - 1, b)

        @block.tensor
        def _(pe):
            pe.wait_ge(w_lo_done, KT)

            def turn(t):
                for b in range(2):
                    pe.wait_ge(m_lo_done[b], t + 1)
                    wait_past(pe, summed[b], t)
                    for n in range(HALVES):
                        cols = slice(n * CW, (n + 1) * CW)
                        for k in range(KT):
                            pe.matmul(acc[b][:, cols], m_hi[:, b, k], w_hi[:, k, cols], start=(k == 0), stop=False)
                            pe.matmul(acc[b][:, cols], m_hi[:, b, k], w_lo[:, k, cols], start=False, stop=False)
                            mm = pe.matmul(acc[b][:, cols], m_lo[:, b, k], w_hi[:, k, cols], start=False,
                                           stop=(k == KT - 1))
                    mm.then_inc(full[b], 1)

            turns_from_first(pe, NT // 2, turn)


def hybrid_block(nc, x, norm_in, w_in, norm_v, w_s, b_s, w_o_gmlp, w_o_sb, w_out, norm_final, out):
    s = {n: nc.dram_tensor(n, [D, S], F32, kind="Internal").ap()
         for n in ("uz_T", "va_T", "q_T", "k_T", "vb_T", "zb_T", "ga_T", "gb_T", "ya_T", "pa_T", "yb_T", "merged_T")}
    norm_and_project(nc, x, norm_in, w_in, s)
    spatial_gating(nc, norm_v, w_s, b_s, s)
    attention(nc, s)
    branch_projection(nc, "a", s["ya_T"], w_o_gmlp, s["ga_T"], None, s["pa_T"])
    branch_projection(nc, "b", s["yb_T"], w_o_sb, s["gb_T"], s["pa_T"], s["merged_T"])
    output_projection(nc, x, w_out, norm_final, out, s)


_INS = ["x", "norm_in", "w_in", "norm_v", "w_s", "b_s", "w_o_gmlp", "w_o_sb", "w_out", "norm_final"]


def kernel(**inputs):
    import numpy as np
    import concourse.bacc as bacc
    from concourse.bass_utils import run_bass_kernel_spmd

    nc = bacc.Bacc("TRN2", target_bir_lowering=False, num_devices=1)
    arrays, args = {}, []
    for name in _INS:
        a = np.ascontiguousarray(inputs[name])
        arrays[f"in_{name}"] = a
        args.append(nc.dram_tensor(f"in_{name}", a.shape, mybir.dt.from_np(a.dtype), kind="ExternalInput").ap())
    out = nc.dram_tensor("out", [1, S, D], F32, kind="ExternalOutput").ap()
    hybrid_block(nc, *args, out)
    r = run_bass_kernel_spmd(nc, [arrays], core_ids=[0])
    return r.results[0]["out"]
```

```python
from contextlib import ExitStack

import concourse.bass as bass
from concourse import mybir
from concourse.alu_op_type import AluOpType as ALU

ACT = mybir.ActivationFunctionType
F32 = mybir.dt.float32
F32R = mybir.dt.float32r

P = 128
D = 1024
S = 2048
KT = D // P
NT = S // P
CW = 512
NC = S // CW
HEADS = 8
GROUPS = 8
EPS = 1e-6
SCALE = float(P) ** -0.5
MASKED = -1e30
WT = 2 * P
BANKS = 8


class Scope:

    def __init__(self, nc, memory, prefix):
        self.nc, self.memory, self.prefix, self.used = nc, memory, prefix, []

    def clear(self):
        self.nc.clear_and_free_semaphores(self.used)
        self.nc.all_engine_barrier()

    def sb(self, name, shape, dt=F32):
        return self.memory.enter_context(self.nc.sbuf_tensor(f"{self.prefix}_{name}", shape, dt))

    def ps(self, name, shape):
        return self.memory.enter_context(self.nc.psum_tensor(f"{self.prefix}_{name}", shape, F32))

    def sem(self, name):
        self.used.append(self.nc.alloc_semaphore(name=f"{self.prefix}_{name}"))
        return self.used[-1]

    def sems(self, name, n):
        return [self.sem(f"{name}{i}") for i in range(n)]


def wait_past(eng, sem, count):
    if not (isinstance(count, int) and count == 0):
        eng.wait_ge(sem, count)


def turns_from_first(eng, turns, body):
    body(0)
    with eng.Fori(1, turns) as t:
        body(t)


class Projection:

    def __init__(self, sc, act_hi, act_lo, banks):
        self.act_hi, self.act_lo, self.banks = act_hi, act_lo, banks
        self.stage = sc.sb("w_stage", [P, 2, KT, WT])
        self.w_hi = sc.sb("w_hi", [P, 2, KT, WT], F32R)
        self.w_lo = sc.sb("w_lo", [P, 2, KT, WT], F32R)
        self.w_loaded = sc.sems("w_loaded", 2)
        self.hi_split = sc.sems("hi_split", 2)
        self.w_ready = sc.sems("w_ready", 2)
        self.full = [sc.sems(f"full{b}_", BANKS) for b in range(2)]
        self.free = sc.sems("free", BANKS)

    def start(self, reader):
        for i in range(BANKS):
            reader.sem_inc(self.free[i], 1)

    def load(self, sp, turn, b, pieces):
        wait_past(sp, self.w_ready[b], turn)
        for dst, src in pieces:
            sp.dma_start(dst, src).then_inc(self.w_loaded[b], 16)

    def by_rows(self, b, weights, at):
        return [(self.stage[:, b, h * KT // 2:(h + 1) * KT // 2, :],
                 weights[:, h * KT // 2:(h + 1) * KT // 2, bass.ds(at, WT)]) for h in range(2)]

    def split(self, dve, turn, b):
        dve.wait_ge(self.w_loaded[b], 32 * turn + 32)
        wait_past(dve, self.full[b][BANKS - 1], turn)
        dve.tensor_copy(self.w_hi[:, b], self.stage[:, b]).then_inc(self.hi_split[b], 1)
        dve.wait_ge(self.hi_split[b], turn + 1)
        dve.tensor_tensor(self.w_lo[:, b], self.stage[:, b], self.w_hi[:, b].bitcast(F32),
                          ALU.subtract).then_inc(self.w_ready[b], 1)

    def multiply(self, pe, turn, b):
        pe.wait_ge(self.w_ready[b], turn + 1)
        for m in range(2):
            for c in range(NC):
                i = m * NC + c
                out, cols, ws = self.banks[i][:, :], slice(c * CW, (c + 1) * CW), slice(m * P, (m + 1) * P)
                pe.wait_ge(self.free[i], 2 * turn + b + 1)
                for k in range(KT):
                    hi, lo = self.w_hi[:, b, k, ws], self.w_lo[:, b, k, ws]
                    pe.matmul(out, hi, self.act_hi[:, k, cols], start=(k == 0), stop=False)
                    pe.matmul(out, hi, self.act_lo[:, k, cols], start=False, stop=False)
                    mm = pe.matmul(out, lo, self.act_hi[:, k, cols], start=False, stop=(k == KT - 1))
                mm.then_inc(self.full[b][i], 1)


def make_identity(pool, ident, zeroed, done):
    pool.memset(ident[:, :], 0.0).then_inc(zeroed, 1)
    pool.wait_ge(zeroed, 1)
    pool.affine_select(out=ident[:, :], in_=ident[:, :], compare_op=ALU.not_equal, fill=1.0, base=0,
                       pattern=[[-1, P]], channel_multiplier=1).then_inc(done, 1)


def norm_and_project(nc, x, norm_in, w_in, s):
    x_t = x.rearrange("a (t p) d -> (a t) p d", p=P)
    w_k = w_in.rearrange("a (k p) f -> p (a k) f", p=P)
    U, VA, ZA, Q, K, VB, ZB, GA, GB = (i * D for i in range(9))
    single = [(VA, ACT.Gelu_apprx_tanh, s["va_T"]), (Q, ACT.Copy, s["q_T"]), (K, ACT.Copy, s["k_T"]),
              (VB, ACT.Copy, s["vb_T"]), (ZB, ACT.Silu, s["zb_T"]), (GA, ACT.Sigmoid, s["ga_T"]),
              (GB, ACT.Sigmoid, s["gb_T"])]
    UZ = KT // 2
    PER = D // WT // 2
    TURNS = UZ + PER * len(single)

    with ExitStack() as memory:
        sc = Scope(nc, memory, "in")
        h_hi = sc.sb("h_hi", [P, KT, S], F32R)
        h_lo = sc.sb("h_lo", [P, KT, S], F32R)
        banks = [sc.ps(f"bank{i}", [P, CW]) for i in range(BANKS)]
        pj = Projection(sc, h_hi, h_lo, banks)
        o_sb = sc.sb("o_sb", [P, BANKS, CW])
        x_sb = sc.sb("x_sb", [P, 2, D])
        gain = sc.sb("gain", [P, D])
        ident = sc.sb("ident", [P, P])
        sq_sum = sc.sb("sq_sum", [P, 2])
        mean_sq = sc.sb("mean_sq", [P, 2])
        inv_rms = sc.sb("inv_rms", [P, 2])
        minus_half = sc.sb("minus_half", [P, 1])

        gain_loaded, zeroed, ident_done, half_set = (
            sc.sem(n) for n in ("gain_loaded", "zeroed", "ident_done", "half_set"))
        x_loaded = sc.sems("x_loaded", 2)
        squared = sc.sems("squared", 2)
        mean_done = sc.sems("mean_done", 2)
        rms_done = sc.sems("rms_done", 2)
        scaled = sc.sems("scaled", 2)
        turned = sc.sems("turned", 2)
        hi_done = sc.sems("hi_done", 2)
        lo_done = sc.sems("lo_done", 2)
        multiplied = sc.sems("multiplied", NC)
        stored = sc.sems("stored", BANKS)
        memory.callback(sc.clear)
        block = memory.enter_context(nc.Block())

        @block.sync
        def _(sp):
            sp.dma_start(x_sb[:, 0], x_t[0]).then_inc(x_loaded[0], 16)
            sp.dma_start(x_sb[:, 1], x_t[1]).then_inc(x_loaded[1], 16)
            sp.dma_start(gain[:, :], norm_in[0:1, :].to_broadcast([P, D])).then_inc(gain_loaded, 16)
            for b in range(2):
                pj.load(sp, 0, b, [(pj.stage[:, b, :, 0:P], w_k[:, :, b * P:(b + 1) * P]),
                                   (pj.stage[:, b, :, P:WT], w_k[:, :, ZA + b * P:ZA + (b + 1) * P])])
            with sp.Fori(1, NT // 2) as t:
                for b in range(2):
                    tile = sp.snap(2 * t + b)
                    sp.wait_ge(turned[b], t)
                    sp.dma_start(x_sb[:, b], x_t[bass.ds(tile, 1)].rearrange("a p d -> p (a d)"))\
                        .then_inc(x_loaded[b], 16)
            with sp.Fori(1, UZ) as t:
                for b in range(2):
                    u_at, z_at = sp.snap(U + (2 * t + b) * P), sp.snap(ZA + (2 * t + b) * P)
                    pj.load(sp, t, b, [(pj.stage[:, b, :, 0:P], w_k[:, :, bass.ds(u_at, P)]),
                                       (pj.stage[:, b, :, P:WT], w_k[:, :, bass.ds(z_at, P)])])
            for n, (at, _, _) in enumerate(single):
                with sp.Fori(0, PER) as t:
                    for b in range(2):
                        w_at = sp.snap(at + (2 * t + b) * WT)
                        pj.load(sp, t + (UZ + n * PER), b, pj.by_rows(b, w_k, w_at))

        @block.gpsimd
        def _(pool):
            pool.memset(minus_half[:, :], -0.5).then_inc(half_set, 1)
            make_identity(pool, ident, zeroed, ident_done)
            pool.wait_ge(half_set, 1)
            with pool.Fori(0, NT // 2) as t:
                for b in range(2):
                    pool.wait_ge(mean_done[b], t + 1)
                    pool.tensor_tensor(inv_rms[:, b:b + 1], mean_sq[:, b:b + 1], minus_half[:, :],
                                       ALU.pow).then_inc(rms_done[b], 1)
            with pool.Fori(0, UZ) as t:
                for b in range(2):
                    for c in range(NC):
                        pool.wait_ge(pj.free[c], 2 * t + b + 2)
                        pool.wait_ge(pj.free[NC + c], 2 * t + b + 2)
                        pool.tensor_tensor(o_sb[:, c], o_sb[:, c], o_sb[:, NC + c], ALU.mult)\
                            .then_inc(multiplied[c], 1)

        @block.scalar
        def _(act):
            def sum_squares(t, b):
                act.wait_ge(x_loaded[b], 16 * t + 16)
                act.activation(o_sb[:, 2 * b:2 * b + 2].rearrange("p a c -> p (a c)"), x_sb[:, b], ACT.Square,
                               accum_out=sq_sum[:, b:b + 1]).then_inc(squared[b], 1)

            def round_hi(t, b, at):
                act.wait_ge(turned[b], t + 1)
                for half in range(2):
                    ins = act.activation(h_hi[:, 4 * half:4 * half + 4, bass.ds(at, P)],
                                         banks[2 * b + half][:, :].rearrange("p (k c) -> p k c", k=4), ACT.Copy)
                ins.then_inc(hi_done[b], 1)

            sum_squares(0, 0)
            with act.Fori(0, NT // 2 - 1) as t:
                sum_squares(t, 1)
                round_hi(t, 0, 2 * t * P)
                sum_squares(t + 1, 0)
                round_hi(t, 1, (2 * t + 1) * P)
            last = NT // 2 - 1
            sum_squares(last, 1)
            round_hi(last, 0, 2 * last * P)
            round_hi(last, 1, (2 * last + 1) * P)

            act.wait_ge(squared[1], NT // 2)

            pj.start(act)

            def gelu_silu(t):
                for b in range(2):
                    row = (2 * t + b) * P
                    for c in range(NC):
                        act.wait_ge(pj.full[b][c], t + 1)
                        wait_past(act, stored[c], 16 * (2 * t + b))
                        act.activation(o_sb[:, c], banks[c][:, :], ACT.Gelu_apprx_tanh).then_inc(pj.free[c], 1)
                    for c in range(NC):
                        i = NC + c
                        act.wait_ge(pj.full[b][i], t + 1)
                        wait_past(act, multiplied[c], 2 * t + b)
                        act.activation(o_sb[:, i], banks[i][:, :], ACT.Silu).then_inc(pj.free[i], 1)
                    for c in range(NC):
                        act.wait_ge(multiplied[c], 2 * t + b + 1)
                        act.dma_start(s["uz_T"][bass.ds(row, P), c * CW:(c + 1) * CW], o_sb[:, c])\
                            .then_inc(stored[c], 16)

            turns_from_first(act, UZ, gelu_silu)
            for n, (_, func, dst) in enumerate(single):
                before = UZ + n * PER

                def one_output(t):
                    for b in range(2):
                        for i in range(BANKS):
                            m, c = divmod(i, NC)
                            row = ((2 * t + b) * 2 + m) * P
                            step = 2 * (t + before) + b
                            act.wait_ge(pj.full[b][i], t + (before + 1))
                            wait_past(act, stored[i], 16 * (step - (0 if i < NC else 2 * UZ)))
                            act.activation(o_sb[:, i], banks[i][:, :], func).then_inc(pj.free[i], 1)
                            act.wait_ge(pj.free[i], step + 2)
                            act.dma_start(dst[bass.ds(row, P), c * CW:(c + 1) * CW], o_sb[:, i])\
                                .then_inc(stored[i], 16)

                if n == 0:
                    turns_from_first(act, PER, one_output)
                else:
                    with act.Fori(0, PER) as t:
                        one_output(t)
            for i in range(BANKS):
                act.wait_ge(stored[i], 16 * 2 * (TURNS if i < NC else TURNS - UZ))

        @block.vector
        def _(dve):
            def mean(t, b):
                dve.wait_ge(squared[b], t + 1)
                dve.tensor_scalar(mean_sq[:, b:b + 1], sq_sum[:, b:b + 1], 1.0 / D, EPS, ALU.mult, ALU.add)\
                    .then_inc(mean_done[b], 1)

            def scale(t, b):
                dve.wait_ge(rms_done[b], t + 1)
                dve.scalar_tensor_tensor(x_sb[:, b], x_sb[:, b], inv_rms[:, b:b + 1], gain[:, :], ALU.mult,
                                         ALU.mult).then_inc(scaled[b], 1)

            def rest_lo(t, b, at):
                dve.wait_ge(hi_done[b], t + 1)
                for half in range(2):
                    ks = slice(4 * half, 4 * half + 4)
                    ins = dve.tensor_tensor(h_lo[:, ks, bass.ds(at, P)],
                                            banks[2 * b + half][:, :].rearrange("p (k c) -> p k c", k=4),
                                            h_hi[:, ks, bass.ds(at, P)].bitcast(F32), ALU.subtract)
                ins.then_inc(lo_done[b], 1)

            for b in range(2):
                dve.sem_inc(lo_done[b], 1)
            dve.wait_ge(gain_loaded, 16)
            mean(0, 0)
            scale(0, 0)
            with dve.Fori(0, NT // 2 - 1) as t:
                mean(t, 1)
                scale(t, 1)
                rest_lo(t, 0, 2 * t * P)
                mean(t + 1, 0)
                scale(t + 1, 0)
                rest_lo(t, 1, (2 * t + 1) * P)
            last = NT // 2 - 1
            mean(last, 1)
            scale(last, 1)
            rest_lo(last, 0, 2 * last * P)
            rest_lo(last, 1, (2 * last + 1) * P)

            def split(t):
                for b in range(2):
                    pj.split(dve, t, b)

            turns_from_first(dve, TURNS, split)

        @block.tensor
        def _(pe):
            pe.wait_ge(ident_done, 1)
            with pe.Fori(0, NT // 2) as t:
                for b in range(2):
                    pe.wait_ge(scaled[b], t + 1)
                    pe.wait_ge(lo_done[b], t + 1)
                    for k in range(KT):
                        ins = pe.transpose(banks[2 * b + k // 4][:, (k % 4) * P:(k % 4 + 1) * P],
                                           x_sb[:, b, k * P:(k + 1) * P], ident[:, :])
                    ins.then_inc(turned[b], 1)
            for b in range(2):
                pe.wait_ge(lo_done[b], NT // 2 + 1)
            with pe.Fori(0, TURNS) as t:
                for b in range(2):
                    pj.multiply(pe, t, b)


PW = 2 * P
PT = PW // P
NPW = S // PW


def split_weight_pieces(act, dve, pieces, loaded, hi_done, lo_done):
    for n, (stage, hi, lo) in enumerate(pieces):
        if act is not None:
            act.wait_ge(loaded[n % 2], 16 * (n // 2 + 1))
            act.activation(hi, stage, ACT.Copy).then_inc(hi_done, 1)
        if dve is not None:
            dve.wait_ge(hi_done, n + 1)
            dve.tensor_tensor(lo, stage, hi.bitcast(F32), ALU.subtract).then_inc(lo_done, 1)


def gate_and_project_a(nc, norm_v, w_s, b_s, w_o_gmlp, s):
    va_n = s["va_T"].rearrange("(g c) s -> c g s", c=P)
    uz_n = s["uz_T"].rearrange("(g c) s -> c g s", c=P)
    ga_k = s["ga_T"].rearrange("(k p) s -> p k s", p=P)
    pa_k = s["pa_T"].rearrange("(k p) s -> p k s", p=P)
    w_k = w_o_gmlp.rearrange("a (k p) f -> p (a k) f", p=P)
    with ExitStack() as memory:
        sc = Scope(nc, memory, "a")
        ident = sc.sb("ident", [P, P])
        w_sb = sc.sb("w_sb", [P, GROUPS, P])
        wT_hi = sc.sb("wT_hi", [P, GROUPS, P], F32R)
        wT_lo = sc.sb("wT_lo", [P, GROUPS, P], F32R)
        bias = sc.sb("bias", [P, GROUPS, P])
        gain = sc.sb("gain", [P, GROUPS])
        va = sc.sb("va", [P, 2, GROUPS, P])
        uz = sc.sb("uz", [P, 2, GROUPS, P])
        v_hi = sc.sb("v_hi", [P, 2, D], F32R)
        v_lo = sc.sb("v_lo", [P, 2, D], F32R)
        y = sc.sb("y", [P, 2, GROUPS, P])
        squares = sc.sb("squares", [P, D])
        sq_sum, mean_sq, inv_rms = (sc.sb(n, [P, 2]) for n in ("sq_sum", "mean_sq", "inv_rms"))
        minus_half = sc.sb("minus_half", [P, 1])
        ya_hi = sc.sb("ya_hi", [P, 2, KT, PW], F32R)
        ya_lo = sc.sb("ya_lo", [P, 2, KT, PW], F32R)
        gate = sc.sb("gate", [P, 2, KT, PW])
        wo_stage = sc.sb("wo_stage", [P, 2, KT, WT])
        wo_hi = sc.sb("wo_hi", [P, KT, D], F32R)
        wo_lo = sc.sb("wo_lo", [P, KT, D], F32R)
        v_ps = sc.ps("v_ps", [P, D])
        m_ps = sc.ps("m_ps", [P, D])
        p_ps = [sc.ps(f"p_ps{n}", [P, CW]) for n in range(4)]

        w_loaded, bias_loaded, gain_loaded, zeroed, ident_done, half_set, masked, w_turned, w_hi_done, w_done = (
            sc.sem(n) for n in ("w_loaded", "bias_loaded", "gain_loaded", "zeroed", "ident_done", "half_set",
                                "masked", "w_turned", "w_hi_done", "w_done"))
        wo_loaded = sc.sems("wo_loaded", 2)
        wo_hi_done, wo_lo_done = sc.sem("wo_hi_done"), sc.sem("wo_lo_done")
        turned, squared, mean_done, rms_done, v_hi_done, v_lo_done, mixed, gained, biased, y_done, y_hi_done, \
            y_lo_done = (sc.sem(n) for n in (
                "turned", "squared", "mean_done", "rms_done", "v_hi_done", "v_lo_done", "mixed", "gained",
                "biased", "y_done", "y_hi_done", "y_lo_done"))
        va_loaded, uz_loaded, gate_loaded, stored = (
            sc.sems(n, 2) for n in ("va_loaded", "uz_loaded", "gate_loaded", "stored"))
        full, gated = sc.sem("full"), sc.sem("gated")
        block = memory.enter_context(nc.Block())

        def per_two_chunks(eng, body):
            body(0, False)
            with eng.Fori(1, NPW // 2 - 1) as t:
                body(t, False)
            body(NPW // 2 - 1, True)

        wo_pieces = [(wo_stage[:, n % 2], wo_hi[:, :, n * WT:(n + 1) * WT], wo_lo[:, :, n * WT:(n + 1) * WT])
                     for n in range(D // WT)]

        @block.sync
        def _(sp):
            def load_tile(tile, b, at):
                first = isinstance(tile, int) and tile < 2
                if not first:
                    sp.wait_ge(turned, tile - 1)
                sp.dma_start(va[:, b], va_n[:, :, bass.ds(at, P)]).then_inc(va_loaded[b], 16)
                if not first:
                    sp.wait_ge(y_done, tile - 1)
                sp.dma_start(uz[:, b], uz_n[:, :, bass.ds(at, P)]).then_inc(uz_loaded[b], 16)

            def snap(x):
                return x if isinstance(x, int) else sp.snap(x)

            sp.dma_start(w_sb[:, :, :], w_s[0].rearrange("g t s -> t g s")).then_inc(w_loaded, 16)
            for n in range(2):
                load_tile(n, n, n * P)
            with nc.allow_non_contiguous_dma(reason="1024 gains, one to a partition"):
                sp.dma_start(gain[:, :], norm_v[0].rearrange("(g c) -> c g", c=P)).then_inc(gain_loaded, 16)
            sp.dma_start(bias[:, :, :].rearrange("p g t -> p (g t)"),
                         b_s.rearrange("a g t -> a (g t)").to_broadcast([P, D])).then_inc(bias_loaded, 16)
            for n, (stage, _, _) in enumerate(wo_pieces):
                if n >= 2:
                    sp.wait_ge(wo_lo_done, n - 1)
                sp.dma_start(stage, w_k[:, :, n * WT:(n + 1) * WT]).then_inc(wo_loaded[n % 2], 16)

            def body(t, last):
                for b in range(2):
                    at = snap((2 * t + b) * PW)
                    ats = [snap((2 * t + b + 1) * PW + n * P) for n in range(PT)]
                    wait_past(sp, stored[b], 16 * t)
                    sp.dma_start(gate[:, b], ga_k[:, :, bass.ds(at, PW)]).then_inc(gate_loaded[b], 16)
                    if not (last and b == 1):
                        for n in range(PT):
                            load_tile(PT * (2 * t + b + 1) + n, n, ats[n])

            per_two_chunks(sp, body)

        @block.gpsimd
        def _(pool):
            pool.memset(minus_half[:, :], -0.5).then_inc(half_set, 1)
            make_identity(pool, ident, zeroed, ident_done)
            pool.wait_ge(w_loaded, 16)
            pool.affine_select(out=w_sb[:, :, :], in_=w_sb[:, :, :], compare_op=ALU.is_ge, fill=0.0, base=0,
                               pattern=[[0, GROUPS], [-1, P]], channel_multiplier=1).then_inc(masked, 1)
            pool.wait_ge(half_set, 1)
            pool.wait_ge(bias_loaded, 16)
            with pool.Fori(0, NT // 2) as t:
                for b in range(2):
                    pool.wait_ge(mean_done, 2 * t + b + 1)
                    pool.tensor_tensor(inv_rms[:, b:b + 1], mean_sq[:, b:b + 1], minus_half[:, :],
                                       ALU.pow).then_inc(rms_done, 1)
                    pool.wait_ge(gained, 2 * t + b + 1)
                    pool.tensor_tensor(y[:, b], y[:, b], bias[:, :, :], ALU.add).then_inc(biased, 1)

        @block.scalar
        def _(act):
            def sum_squares(tile, b):
                act.wait_ge(turned, tile + 1)
                act.activation(squares[:, :], v_ps[:, :], ACT.Square,
                               accum_out=sq_sum[:, b:b + 1]).then_inc(squared, 1)

            def round_v(tile, b):
                act.wait_ge(rms_done, tile + 1)
                if not isinstance(tile, int) or tile >= 2:
                    act.wait_ge(mixed, tile - 1)
                act.activation(v_hi[:, b], v_ps[:, :], ACT.Copy, scale=inv_rms[:, b:b + 1])\
                    .then_inc(v_hi_done, 1)

            def round_y(tile, b, chunk, cb):
                act.wait_ge(y_done, tile + 1)
                if not isinstance(chunk, int) or chunk >= 2:
                    act.wait_ge(full, KT * chunk - KT)
                act.activation(ya_hi[:, cb, :, b * P:(b + 1) * P], y[:, b], ACT.Copy).then_inc(y_hi_done, 1)

            act.wait_ge(w_turned, 1)
            act.activation(wT_hi[:, :, :].rearrange("p g t -> p (g t)"), m_ps[:, :], ACT.Copy).then_inc(w_hi_done, 1)
            for n in range(PT):
                sum_squares(n, n)
                round_v(n, n)
                round_y(n, n, 0, 0)
            split_weight_pieces(act, None, wo_pieces, wo_loaded, wo_hi_done, None)

            def body(t, last):
                for b in range(2):
                    chunk = 2 * t + b
                    if not (last and b == 1):
                        nxt = PT * (chunk + 1)
                        sum_squares(nxt, 0)
                        round_v(nxt, 0)
                        sum_squares(nxt + 1, 1)
                        round_y(nxt, 0, chunk + 1, 1 - b)
                        round_v(nxt + 1, 1)
                        round_y(nxt + 1, 1, chunk + 1, 1 - b)
                    at = chunk * PW
                    act.wait_ge(gated, KT * chunk + KT)
                    act.dma_start(pa_k[:, :, bass.ds(at, PW)], gate[:, b]).then_inc(stored[b], 16)

            per_two_chunks(act, body)
            for b in range(2):
                act.wait_ge(stored[b], 16 * (NPW // 2))

        @block.vector
        def _(dve):
            def mean(tile, b):
                dve.wait_ge(squared, tile + 1)
                dve.tensor_scalar(mean_sq[:, b:b + 1], sq_sum[:, b:b + 1], 1.0 / D, EPS, ALU.mult,
                                  ALU.add).then_inc(mean_done, 1)

            def rest_v(tile, b):
                dve.wait_ge(v_hi_done, tile + 1)
                dve.scalar_tensor_tensor(v_lo[:, b], v_ps[:, :], inv_rms[:, b:b + 1],
                                         v_hi[:, b].bitcast(F32), ALU.mult, ALU.subtract).then_inc(v_lo_done, 1)

            def gain_mix(tile, b):
                dve.wait_ge(mixed, tile + 1)
                dve.tensor_tensor(y[:, b], m_ps[:, :].rearrange("p (g t) -> p g t", g=GROUPS),
                                  gain[:, :].unsqueeze(2).to_broadcast([P, GROUPS, P]), ALU.mult)\
                    .then_inc(gained, 1)

            def times_uz(tile, b, loads):
                dve.wait_ge(biased, tile + 1)
                dve.wait_ge(uz_loaded[b], 16 * loads)
                dve.tensor_tensor(y[:, b], y[:, b], uz[:, b], ALU.mult).then_inc(y_done, 1)

            def rest_y(tile, b, cb):
                dve.wait_ge(y_hi_done, tile + 1)
                dve.tensor_tensor(ya_lo[:, cb, :, b * P:(b + 1) * P], y[:, b],
                                  ya_hi[:, cb, :, b * P:(b + 1) * P].bitcast(F32), ALU.subtract)\
                    .then_inc(y_lo_done, 1)

            dve.wait_ge(w_hi_done, 1)
            dve.tensor_tensor(wT_lo[:, :, :].rearrange("p g t -> p (g t)"), m_ps[:, :],
                              wT_hi[:, :, :].rearrange("p g t -> p (g t)").bitcast(F32), ALU.subtract)\
                .then_inc(w_done, 1)
            dve.wait_ge(gain_loaded, 16)
            for n in range(PT):
                mean(n, n)
                rest_v(n, n)
                gain_mix(n, n)
                times_uz(n, n, 1)
                rest_y(n, n, 0)
            split_weight_pieces(None, dve, wo_pieces, None, wo_hi_done, wo_lo_done)

            def body(t, last):
                for b in range(2):
                    chunk = 2 * t + b

                    def apply_gate(k):
                        if k == 0:
                            dve.wait_ge(gate_loaded[b], 16 * t + 16)
                        dve.wait_ge(full, KT * chunk + (k + 1))
                        dve.tensor_tensor(gate[:, b, k], p_ps[k % 4][:, 0:PW], gate[:, b, k], ALU.mult)\
                            .then_inc(gated, 1)

                    if last and b == 1:
                        for k in range(KT):
                            apply_gate(k)
                        continue
                    nxt, cb = PT * (chunk + 1), 1 - b
                    mean(nxt, 0)
                    apply_gate(0)
                    rest_v(nxt, 0)
                    apply_gate(1)
                    gain_mix(nxt, 0)
                    apply_gate(2)
                    times_uz(nxt, 0, chunk + 2)
                    mean(nxt + 1, 1)
                    apply_gate(3)
                    rest_y(nxt, 0, cb)
                    rest_v(nxt + 1, 1)
                    apply_gate(4)
                    gain_mix(nxt + 1, 1)
                    apply_gate(5)
                    times_uz(nxt + 1, 1, chunk + 2)
                    apply_gate(6)
                    rest_y(nxt + 1, 1, cb)
                    apply_gate(7)

            per_two_chunks(dve, body)

        @block.tensor
        def _(pe):
            def turn(tile, b, loads):
                pe.wait_ge(va_loaded[b], 16 * loads)
                wait_past(pe, v_lo_done, tile)
                for g in range(GROUPS):
                    ins = pe.transpose(v_ps[:, g * P:(g + 1) * P], va[:, b, g, :], ident[:, :])
                ins.then_inc(turned, 1)

            def mix(tile, b):
                pe.wait_ge(v_lo_done, tile + 1)
                wait_past(pe, gained, tile)
                for g in range(GROUPS):
                    gs = slice(g * P, (g + 1) * P)
                    pe.matmul(m_ps[:, gs], v_hi[:, b, gs], wT_hi[:, g], start=True, stop=False)
                    pe.matmul(m_ps[:, gs], v_hi[:, b, gs], wT_lo[:, g], start=False, stop=False)
                    mm = pe.matmul(m_ps[:, gs], v_lo[:, b, gs], wT_hi[:, g], start=False, stop=True)
                mm.then_inc(mixed, 1)

            pe.wait_ge(ident_done, 1)
            pe.wait_ge(masked, 1)
            for g in range(GROUPS):
                ins = pe.transpose(m_ps[:, g * P:(g + 1) * P], w_sb[:, g, :], ident[:, :])
            ins.then_inc(w_turned, 1)
            turn(0, 0, 1)
            pe.wait_ge(w_done, 1)
            mix(0, 0)
            turn(1, 1, 1)
            mix(1, 1)

            def body(t, last):
                for b in range(2):
                    chunk = 2 * t + b

                    def project(k):
                        if k == 0:
                            pe.wait_ge(y_lo_done, PT * chunk + PT)
                        if isinstance(chunk, int) and chunk == 0 and k % 2 == 0:
                            pe.wait_ge(wo_lo_done, k // 2 + 1)
                        if not (isinstance(chunk, int) and chunk == 0 and k < 4):
                            pe.wait_ge(gated, KT * chunk + (k - 3))
                        out, ks = p_ps[k % 4][:, 0:PW], slice(k * P, (k + 1) * P)
                        for j in range(KT):
                            pe.matmul(out, wo_hi[:, j, ks], ya_hi[:, b, j], start=(j == 0), stop=False)
                            pe.matmul(out, wo_hi[:, j, ks], ya_lo[:, b, j], start=False, stop=False)
                            mm = pe.matmul(out, wo_lo[:, j, ks], ya_hi[:, b, j], start=False, stop=(j == KT - 1))
                        mm.then_inc(full, 1)

                    nxt = PT * (chunk + 1)
                    mixes = {} if last and b == 1 else {
                        0: lambda: turn(nxt, 0, chunk + 2), 2: lambda: mix(nxt, 0),
                        3: lambda: turn(nxt + 1, 1, chunk + 2), 5: lambda: mix(nxt + 1, 1)}
                    for k in range(KT):
                        if k in mixes:
                            mixes[k]()
                        project(k)

            per_two_chunks(pe, body)


QT = CW // P
NSUP = NT // QT
ZW = CW
Z_BANKS = 4
AHEAD = 2
T_BANKS = 3
QK_WEIGHT, QK_REST = 8, 14


def blend(some, others):
    def spread(which, events):
        total, so_far = sum(w for _, w in events), 0
        for e, w in events:
            yield (so_far + w / 2) / total, which, e
            so_far += w

    return [e for _, _, e in sorted([*spread(0, some), *spread(1, others)], key=lambda a: a[:2])]


def z_pieces(sup):
    return [("Z", i, at, min(ZW, (i + 1) * P - at)) for i in range(sup * QT, (sup + 1) * QT)
            for at in reversed(range(0, (i + 1) * P, ZW))]


def b_steps(sup):
    return [("B", sup, kt) for kt in range((sup + 1) * QT)]


def head_order(last):
    products = [(("V", g), 1) for g in range(NT // QT)]
    products += [(e, min(QT, QT * (e[1] + 1) - e[2])) for sup in range(NSUP) for e in b_steps(sup)]
    ahead = [(e, e[3] // P) for e in z_pieces(NSUP - 1)]
    if not last:
        ahead += [(("QK", part), QK_WEIGHT / 4) for part in range(4)] + [(None, QK_REST)]
        ahead += [(e, e[3] // P) for sup in range(NSUP - 1) for e in z_pieces(sup)]
    else:
        ahead += [(None, QK_WEIGHT + QK_REST + sum(e[3] // P for sup in range(NSUP - 1) for e in z_pieces(sup)))]
    order, pending = [], []
    for e in blend(ahead, products):
        kind = None if e is None else e[0]
        if kind == "Z":
            order += [e] + pending
            pending = [("W", *e[1:])]
            continue
        if kind in (None, "QK") or e[:2] == ("B", NSUP - 1):
            order += pending
            pending = []
        if kind is not None:
            order.append(e)
    order += pending
    out, waiting = [], []

    def product():
        _, sup, kt = waiting.pop(0)
        out.append(("P", sup, kt))
        if kt == len(b_steps(sup)) - 1:
            out.append(("Y", sup))

    for e in order:
        out.append(e)
        if e[0] == "B":
            waiting.append(e)
            if len(waiting) > AHEAD:
                product()
    while waiting:
        product()
    return out


def places(order):
    seen = dict.fromkeys("ZWTP", 0)
    for e in order:
        kind = {"V": "T", "B": "T"}.get(e[0], e[0])
        yield e, seen.get(kind)
        if kind in seen:
            seen[kind] += 1


def attention(nc, s):
    PIECES = sum(len(z_pieces(n)) for n in range(NSUP))
    PRODUCTS = sum(len(b_steps(n)) for n in range(NSUP))
    STEPS = NT // QT + PRODUCTS
    FIRST = sum(len(z_pieces(n)) for n in range(NSUP - 1))
    BY_DVE = [3]
    W_BUFS = 4
    assert PIECES % Z_BANKS == 0 and PRODUCTS % W_BUFS == 0

    with ExitStack() as memory:
        sc = Scope(nc, memory, "att")
        ident = sc.sb("ident", [P, P])
        ident_r = sc.sb("ident_r", [P, P], F32R)
        mask = sc.sb("mask", [P, P])
        mask_r = sc.sb("mask_r", [P, P], F32R)
        q_in, k_in, v_in = (sc.sb(n, [P, S]) for n in ("q_in", "k_in", "v_in"))
        q_hi, q_lo, k_hi, k_lo = (sc.sb(n, [P, S], F32R) for n in ("q_hi", "q_lo", "k_hi", "k_lo"))
        v = sc.sb("v", [P, S])
        slot = [sc.sb(f"slot{n}", [P, (n + 1) * P]) for n in range(NT)]
        rest = [sc.sb(f"rest{n}", [P, S + 1]) for n in range(2)]
        wT = [sc.sb(f"wT{n}", [P, CW]) for n in range(W_BUFS)]
        zb = [sc.sb(f"zb{n}", [P, CW]) for n in range(2)]
        y = [sc.sb(f"y{n}", [P, CW]) for n in range(2)]
        z_ps = [sc.ps(f"z_ps{n}", [P, ZW]) for n in range(Z_BANKS)]
        t_ps = [sc.ps(f"t_ps{n}", [P, CW]) for n in range(T_BANKS)]
        y_ps = sc.ps("y_ps", [P, CW])

        zeroed, ident_done, mask_zeroed, mask_done, consts, ones_set = (
            sc.sem(n) for n in ("zeroed", "ident_done", "mask_zeroed", "mask_done", "consts", "ones_set"))
        qk_loaded, v_loaded = sc.sem("qk_loaded"), sc.sem("v_loaded")
        qk_hi, qk_done = sc.sem("qk_hi"), sc.sem("qk_done")
        z_full = sc.sem("z_full")
        z_read = sc.sems("z_read", Z_BANKS)
        scanned = sc.sem("scanned")
        weighted = sc.sem("weighted")
        turned = sc.sem("turned")
        copied_a, copied_d = sc.sem("copied_a"), sc.sem("copied_d")
        product = sc.sem("product")
        zb_loaded, y_done, stored = (sc.sems(n, 2) for n in ("zb_loaded", "y_done", "stored"))
        block = memory.enter_context(nc.Block())

        kinds = [e for e, _ in places(head_order(False)) if e[0] in "VB"]

        def by_dve(t):
            return t in BY_DVE

        def t_bank(t):
            return t_ps[t % T_BANKS]

        def bank_before(t):
            return max(n for n in range(-STEPS, t) if n % STEPS % T_BANKS == t % T_BANKS)

        def copied(eng, h, t):
            mine = by_dve(t % STEPS)
            a_head = sum(by_dve(n) == mine for n in range(STEPS))
            done = sum(by_dve(n) == mine for n in range(t % STEPS + 1))
            if t < 0:
                if isinstance(h, int) and h == 0:
                    return
                done -= a_head
            eng.wait_ge(copied_d if mine else copied_a, a_head * h + done)

        def product_of(e):
            return [k for k in kinds if k[0] == "B"].index(e)

        def buffer_free(eng, h, k):
            if not isinstance(h, int) or PRODUCTS * h + k >= W_BUFS:
                eng.wait_ge(product, PRODUCTS * h + (k - W_BUFS + 1))

        def steps_until(sup):
            return max(n + 1 for n, e in enumerate(kinds) if e[:2] == ("B", sup))

        V_READ = max(n + 1 for n, e in enumerate(kinds) if e[0] == "V")
        ALL = [e for n in range(NSUP) for e in z_pieces(n)]

        early = ALL[:FIRST]

        def pieces_before(i):
            return sum(e[1] < i for e in ALL)

        def quarter(part):
            cols = slice(part % 2 * S // 2, (part % 2 + 1) * S // 2)
            return ((q_in, q_hi, q_lo), (k_in, k_hi, k_lo))[part // 2], cols

        def first_head(h):
            return isinstance(h, int) and h == 0

        def products_until(sup):
            return sum(len(b_steps(n)) for n in range(sup + 1))

        def per_head(eng, body):
            body(0, False)
            with eng.Fori(1, HEADS - 1) as h:
                body(h, False)
            body(HEADS - 1, True)

        @block.sync
        def _(sp):
            def load_qk(h):
                row = h * P if isinstance(h, int) else sp.snap(h * P)
                if not isinstance(h, int) or h > 0:
                    sp.wait_ge(qk_done, 4 * h)
                sp.dma_start(q_in[:, :], s["q_T"][bass.ds(row, P), :]).then_inc(qk_loaded, 16)
                sp.dma_start(k_in[:, :], s["k_T"][bass.ds(row, P), :]).then_inc(qk_loaded, 16)

            def body(h, last):
                row = h * P if isinstance(h, int) else sp.snap(h * P)
                nxt = (h + 1) * P if isinstance(h, int) else sp.snap((h + 1) * P)
                if not last:
                    load_qk(h + 1)
                for sup in range(NSUP):
                    n = sup % 2
                    cols = slice(sup * CW, (sup + 1) * CW)
                    wait_past(sp, y_done[n], 2 * h + sup // 2)
                    sp.dma_start(zb[n][:, :], s["zb_T"][bass.ds(row, P), cols]).then_inc(zb_loaded[n], 16)
                    if sup >= 1:
                        m = (sup - 1) % 2
                        sp.wait_ge(y_done[m], 2 * h + ((sup - 1) // 2 + 1))
                        sp.dma_start(s["yb_T"][bass.ds(row, P), (sup - 1) * CW:sup * CW], y[m][:, :])\
                            .then_inc(stored[m], 16)
                    if sup == 0 and not last:
                        sp.wait_ge(turned, STEPS * h + V_READ)
                        sp.dma_start(v_in[:, :], s["vb_T"][bass.ds(nxt, P), :]).then_inc(v_loaded, 16)
                sp.wait_ge(y_done[1], 2 * h + 2)
                sp.dma_start(s["yb_T"][bass.ds(row, P), (NSUP - 1) * CW:], y[1][:, :]).then_inc(stored[1], 16)

            load_qk(0)
            sp.dma_start(v_in[:, :], s["vb_T"][0:P, :]).then_inc(v_loaded, 16)
            per_head(sp, body)
            for n in range(2):
                sp.wait_ge(stored[n], 16 * 2 * HEADS)

        @block.gpsimd
        def _(pool):
            make_identity(pool, ident, zeroed, ident_done)
            pool.memset(mask[:, :], 0.0).then_inc(mask_zeroed, 1)
            pool.wait_ge(mask_zeroed, 1)
            pool.affine_select(out=mask[:, :], in_=mask[:, :], compare_op=ALU.is_gt, fill=MASKED, base=0,
                               pattern=[[-1, P]], channel_multiplier=1).then_inc(mask_done, 1)

        @block.scalar
        def _(act):
            def split_qk(h, part):
                if part == 0:
                    act.wait_ge(qk_loaded, 32 * h + 32)
                    wait_past(act, z_full, PIECES * h)
                (src, hi, _), cols = quarter(part)
                act.activation(hi[:, cols], src[:, cols], ACT.Copy).then_inc(qk_hi, 1)

            def sigmoids(i, at, width, h, n):
                src = z_ps[n % Z_BANKS][:, 0:width]
                w = (i + 1) * P
                right = S - w + at
                act.wait_ge(z_full, PIECES * h + (n + 1))
                if at + width == w:
                    if not first_head(h):
                        act.wait_ge(turned, STEPS * h + (steps_until(i // QT) - STEPS))
                act.activation(slot[i][:, at:at + width], src, ACT.Sigmoid, scale=SCALE)
                if at + width == w:
                    if i >= 2:
                        act.wait_ge(weighted, PIECES * h + pieces_before(i - 1))
                    elif not first_head(h):
                        act.wait_ge(weighted, PIECES * h + (pieces_before(NT + i - 1) - PIECES))
                act.activation(rest[i % 2][:, right:right + width], src, ACT.Sigmoid, scale=-SCALE)\
                    .then_inc(z_read[n % Z_BANKS], 1)

            def body(h, last):
                for e, n in places(head_order(last)):
                    if e[0] == "Z" and e[1] >= NT - QT:
                        sigmoids(*e[1:], h, FIRST + n)
                    elif e[0] == "Z":
                        sigmoids(*e[1:], h + 1, FIRST + n - PIECES)
                    elif e[0] == "QK":
                        split_qk(h + 1, e[1])
                    elif e[0] in "VB" and not by_dve(n):
                        copy_out(act, h, e, n, copied_a)

            def copy_out(act, h, e, t, done):
                act.wait_ge(turned, STEPS * h + (t + 1))
                if e[0] == "V":
                    wait_past(act, product, PRODUCTS * h)
                    act.activation(v[:, e[1] * CW:(e[1] + 1) * CW], t_bank(t)[:, :],
                                   ACT.Copy).then_inc(done, 1)
                else:
                    k, c0 = product_of(e), max(0, e[2] - QT * e[1]) * P
                    buffer_free(act, h, k)
                    act.activation(wT[k % W_BUFS][:, c0:], t_bank(t)[:, c0:], ACT.Copy).then_inc(done, 1)

            for part in range(4):
                split_qk(0, part)
            act.wait_ge(ones_set, 2)
            for n, e in enumerate(early):
                sigmoids(*e[1:], 0, n)
            per_head(act, body)

        @block.vector
        def _(dve):
            def split_qk(h, part):
                dve.wait_ge(qk_hi, 4 * h + part + 1)
                (src, hi, lo), cols = quarter(part)
                dve.tensor_tensor(lo[:, cols], src[:, cols], hi[:, cols].bitcast(F32), ALU.subtract)\
                    .then_inc(qk_done, 1)

            def weights(i, at, width, h, n):
                dve.wait_ge(z_read[n % Z_BANKS], PIECES // Z_BANKS * h + (n // Z_BANKS + 1))
                left = S - (i + 1) * P + at
                r = rest[i % 2]
                backwards = r[:, left:left + width][:, ::-1]
                dve.tensor_tensor_scan(out=backwards, data0=backwards, data1=backwards,
                                       initial=r[:, left + width:left + width + 1], op0=ALU.mult,
                                       op1=ALU.bypass).then_inc(scanned, 1)
                dve.wait_ge(scanned, PIECES * h + (n + 1))
                a = slot[i][:, at:at + width]
                dve.tensor_tensor(a, a, r[:, left + 1:left + width + 1], ALU.mult).then_inc(weighted, 1)

            def body(h, last):
                for e, n in places(head_order(last)):
                    if e[0] == "W" and e[1] >= NT - QT:
                        weights(*e[1:], h, FIRST + n)
                    elif e[0] == "W":
                        weights(*e[1:], h + 1, FIRST + n - PIECES)
                    elif e[0] == "QK":
                        split_qk(h + 1, e[1])
                    elif e[0] in "VB" and by_dve(n):
                        dve.wait_ge(turned, STEPS * h + (n + 1))
                        if e[0] == "V":
                            wait_past(dve, product, PRODUCTS * h)
                            dve.tensor_copy(v[:, e[1] * CW:(e[1] + 1) * CW], t_bank(n)[:, :]).then_inc(copied_d, 1)
                        else:
                            k, c0 = product_of(e), max(0, e[2] - QT * e[1]) * P
                            buffer_free(dve, h, k)
                            dve.tensor_copy(wT[k % W_BUFS][:, c0:], t_bank(n)[:, c0:]).then_inc(copied_d, 1)
                    elif e[0] == "Y":
                        sup, m = e[1], e[1] % 2
                        dve.wait_ge(product, PRODUCTS * h + products_until(sup))
                        dve.wait_ge(zb_loaded[m], 32 * h + 16 * (sup // 2 + 1))
                        wait_past(dve, stored[m], 32 * h + 16 * (sup // 2))
                        dve.tensor_tensor(y[m][:, :], y_ps[:, :], zb[m][:, :], ALU.mult).then_inc(y_done[m], 1)

            dve.memset(rest[0][:, S:S + 1], 1.0).then_inc(ones_set, 1)
            dve.memset(rest[1][:, S:S + 1], 1.0).then_inc(ones_set, 1)
            dve.wait_ge(ident_done, 1)
            dve.tensor_copy(ident_r[:, :], ident[:, :]).then_inc(consts, 1)
            dve.wait_ge(mask_done, 1)
            dve.tensor_copy(mask_r[:, :], mask[:, :]).then_inc(consts, 1)
            for part in range(4):
                split_qk(0, part)
            for n, e in enumerate(early):
                weights(*e[1:], 0, n)
            per_head(dve, body)

        @block.tensor
        def _(pe):
            def logits(i, at, width, h, n):
                wait_past(pe, z_read[n % Z_BANKS], PIECES // Z_BANKS * h + n // Z_BANKS)
                qs = slice(i * P, (i + 1) * P)
                out, ks = z_ps[n % Z_BANKS][:, 0:width], slice(at, at + width)
                diagonal = at + width == (i + 1) * P
                pe.matmul(out, q_hi[:, qs], k_hi[:, ks], start=True, stop=False)
                pe.matmul(out, q_hi[:, qs], k_lo[:, ks], start=False, stop=False)
                mm = pe.matmul(out, q_lo[:, qs], k_hi[:, ks], start=False, stop=not diagonal)
                if diagonal:
                    mm = pe.matmul(z_ps[n % Z_BANKS][:, width - P:width], ident_r[:, :], mask_r[:, :],
                                   start=False, stop=True)
                mm.then_inc(z_full, 1)

            def body(h, last):
                for e, n in places(head_order(last)):
                    if e[0] == "Z" and e[1] >= NT - QT:
                        logits(*e[1:], h, FIRST + n)
                    elif e[0] == "Z":
                        if e[1] == 0:
                            pe.wait_ge(qk_done, 4 * h + 8)
                        logits(*e[1:], h + 1, FIRST + n - PIECES)
                    elif e[0] in "VB":
                        copied(pe, h, bank_before(n))
                        bank = t_bank(n)
                        if e == ("V", 0):
                            pe.wait_ge(v_loaded, 16 * h + 16)
                        for j in range(QT):
                            out = bank[:, j * P:(j + 1) * P]
                            if e[0] == "V":
                                at = (e[1] * QT + j) * P
                                ins = pe.transpose(out, v_in[:, at:at + P], ident[:, :])
                            elif e[2] <= QT * e[1] + j:
                                i, kt = QT * e[1] + j, e[2]
                                if kt == 0:
                                    pe.wait_ge(weighted, PIECES * h + pieces_before(i + 1))
                                ins = pe.transpose(out, slot[i][:, kt * P:(kt + 1) * P], ident[:, :])
                        ins.then_inc(turned, 1)
                    elif e[0] == "P":
                        _, sup, kt = e
                        c0 = max(0, kt - QT * sup) * P
                        copied(pe, h, kinds.index(("B", sup, kt)))
                        if kt == 0:
                            wait_past(pe, y_done[(sup - 1) % 2], 2 * h + (sup + 1) // 2)
                        if (sup, kt) == (0, 0):
                            own = by_dve(kinds.index(("B", sup, kt)))
                            copied(pe, h, max(t for t, k in enumerate(kinds) if k[0] == "V" and by_dve(t) != own))
                        pe.matmul(y_ps[:, c0:], v[:, kt * P:(kt + 1) * P], wT[n % W_BUFS][:, c0:],
                                  start=(kt == 0), stop=(kt == len(b_steps(sup)) - 1)).then_inc(product, 1)

            pe.wait_ge(consts, 2)
            pe.wait_ge(qk_done, 4)
            for n, e in enumerate(early):
                logits(*e[1:], 0, n)
            per_head(pe, body)


def merge_and_project_out(nc, x, w_o_sb, w_out, norm_final, out, s):
    x_t = x.rearrange("a (t p) d -> (a t) p d", p=P)
    out_t = out.rearrange("a (t p) d -> (a t) p d", p=P)
    yb_k, gb_k, pa_k = (s[n].rearrange("(k p) s -> p k s", p=P) for n in ("yb_T", "gb_T", "pa_T"))
    wo_k, wf_k = (w.rearrange("a (k p) f -> p (a k) f", p=P) for w in (w_o_sb, w_out))
    HALVES = D // CW
    with ExitStack() as memory:
        sc = Scope(nc, memory, "b")
        wo_hi, wo_lo, wf_hi, wf_lo = (sc.sb(n, [P, KT, D], F32R) for n in ("wo_hi", "wo_lo", "wf_hi", "wf_lo"))
        y_in = sc.sb("y_in", [P, KT, PW])
        y_hi = sc.sb("y_hi", [P, KT, PW], F32R)
        y_lo = sc.sb("y_lo", [P, KT, PW], F32R)
        gate = sc.sb("gate", [P, KT, PW])
        pa = sc.sb("pa", [P, KT, PW])
        m_hi = sc.sb("m_hi", [P, KT, PW], F32R)
        m_lo = sc.sb("m_lo", [P, KT, PW], F32R)
        x_sb = sc.sb("x_sb", [P, PT, D])
        o_sb = sc.sb("o_sb", [P, PT, D])
        gain = sc.sb("gain", [P, D])
        sq_sum, mean_sq, inv_rms = (sc.sb(n, [P, PT]) for n in ("sq_sum", "mean_sq", "inv_rms"))
        minus_half = sc.sb("minus_half", [P, 1])
        p_ps = [sc.ps(f"p_ps{n}", [P, CW]) for n in range(4)]
        acc = [sc.ps(f"acc{n}", [P, D]) for n in range(PT)]

        gain_loaded, half_set = sc.sem("gain_loaded"), sc.sem("half_set")
        w_loaded = sc.sems("w_loaded", 2)
        w_hi_done, w_lo_done = sc.sem("w_hi_done"), sc.sem("w_lo_done")
        y_loaded, gate_loaded, pa_loaded = (sc.sem(n) for n in ("y_loaded", "gate_loaded", "pa_loaded"))
        y_hi_done, y_lo_done = sc.sem("y_hi_done"), sc.sem("y_lo_done")
        full, gated, merged, m_hi_done, m_lo_done = (
            sc.sem(n) for n in ("full", "gated", "merged", "m_hi_done", "m_lo_done"))
        x_loaded, full_out, summed, squared, mean_done, rms_done, o_done, stored = (
            sc.sems(n, PT) for n in ("x_loaded", "full_out", "summed", "squared", "mean_done", "rms_done",
                                     "o_done", "stored"))
        block = memory.enter_context(nc.Block())
        stages = [t[:, :, :].rearrange("p a d -> p (a d)").rearrange("p (k f) -> p k f", k=KT) for t in (x_sb, o_sb)]
        w_pieces_ = [(stages[n % 2], hi[:, :, m * WT:(m + 1) * WT], lo[:, :, m * WT:(m + 1) * WT])
                     for n, (hi, lo, m) in enumerate([(wo_hi, wo_lo, m) for m in range(D // WT)] +
                                                     [(wf_hi, wf_lo, m) for m in range(D // WT)])]
        sources = [(w, m) for w in (wo_k, wf_k) for m in range(D // WT)]
        N_PIECES = len(sources)

        @block.sync
        def _(sp):
            def snap(v):
                return v if isinstance(v, int) else sp.snap(v)

            def load_x(c, n, tile):
                wait_past(sp, o_done[n], c)
                sp.dma_start(x_sb[:, n], x_t[bass.ds(tile, 1)].rearrange("a p d -> p (a d)"))\
                    .then_inc(x_loaded[n], 16)

            def load_chunk(c, at):
                wait_past(sp, y_lo_done, c)
                sp.dma_start(y_in[:, :, :], yb_k[:, :, bass.ds(at, PW)]).then_inc(y_loaded, 16)
                wait_past(sp, m_lo_done, KT * c)
                sp.dma_start(gate[:, :, :], gb_k[:, :, bass.ds(at, PW)]).then_inc(gate_loaded, 16)
                wait_past(sp, merged, KT * c)
                sp.dma_start(pa[:, :, :], pa_k[:, :, bass.ds(at, PW)]).then_inc(pa_loaded, 16)

            for n, (w, m) in enumerate(sources):
                if n >= 2:
                    sp.wait_ge(w_lo_done, n - 1)
                sp.dma_start(stages[n % 2], w[:, :, m * WT:(m + 1) * WT]).then_inc(w_loaded[n % 2], 16)
                if n == 0:
                    load_chunk(0, 0)
            sp.dma_start(gain[:, :], norm_final.unsqueeze(0).to_broadcast([P, D])).then_inc(gain_loaded, 16)
            sp.wait_ge(w_lo_done, N_PIECES)
            for n in range(PT):
                load_x(0, n, n)

            with sp.Fori(1, NPW) as c:
                at, tiles = snap(c * PW), [snap(PT * c + n) for n in range(PT)]
                load_chunk(c, at)
                for n in range(PT):
                    load_x(c, n, tiles[n])

        @block.gpsimd
        def _(pool):
            pool.memset(minus_half[:, :], -0.5).then_inc(half_set, 1)
            pool.wait_ge(half_set, 1)
            with pool.Fori(0, NPW) as c:
                for n in range(PT):
                    pool.wait_ge(mean_done[n], c + 1)
                    pool.tensor_tensor(inv_rms[:, n:n + 1], mean_sq[:, n:n + 1], minus_half[:, :],
                                       ALU.pow).then_inc(rms_done[n], 1)

        @block.scalar
        def _(act):
            def round_y(c):
                act.wait_ge(y_loaded, 16 * c + 16)
                wait_past(act, full, KT * c)
                act.activation(y_hi[:, :, :], y_in[:, :, :], ACT.Copy).then_inc(y_hi_done, 1)

            def body(c, last):
                for k in range(KT):
                    act.wait_ge(merged, KT * c + (k + 1))
                    if k == 0:
                        for n in range(PT):
                            wait_past(act, full_out[n], c)
                    act.activation(m_hi[:, k], gate[:, k], ACT.Copy).then_inc(m_hi_done, 1)
                if not last:
                    round_y(c + 1)
                for n in range(PT):
                    act.wait_ge(summed[n], c + 1)
                    wait_past(act, stored[n], 16 * c)
                    act.activation(o_sb[:, n], x_sb[:, n], ACT.Square, accum_out=sq_sum[:, n:n + 1])\
                        .then_inc(squared[n], 1)
                for n in range(PT):
                    act.wait_ge(o_done[n], c + 1)
                    act.dma_start(out_t[bass.ds(PT * c + n, 1)].rearrange("a p d -> p (a d)"), o_sb[:, n])\
                        .then_inc(stored[n], 16)

            round_y(0)
            split_weight_pieces(act, None, w_pieces_, w_loaded, w_hi_done, None)
            body(0, False)
            with act.Fori(1, NPW - 1) as c:
                body(c, False)
            body(NPW - 1, True)
            for n in range(PT):
                act.wait_ge(stored[n], 16 * NPW)

        @block.vector
        def _(dve):
            def rest_y(c):
                dve.wait_ge(y_hi_done, c + 1)
                dve.tensor_tensor(y_lo[:, :, :], y_in[:, :, :], y_hi[:, :, :].bitcast(F32), ALU.subtract)\
                    .then_inc(y_lo_done, 1)

            def body(c, last):
                def rest_m(k):
                    dve.wait_ge(m_hi_done, KT * c + (k + 1))
                    dve.tensor_tensor(m_lo[:, k], gate[:, k], m_hi[:, k].bitcast(F32), ALU.subtract)\
                        .then_inc(m_lo_done, 1)

                dve.wait_ge(gate_loaded, 16 * c + 16)
                dve.wait_ge(pa_loaded, 16 * c + 16)
                for k in range(KT):
                    dve.wait_ge(full, KT * c + (k + 1))
                    dve.tensor_tensor(gate[:, k], p_ps[k % 4][:, 0:PW], gate[:, k], ALU.mult).then_inc(gated, 1)
                    dve.wait_ge(gated, KT * c + (k + 1))
                    dve.tensor_tensor(gate[:, k], gate[:, k], pa[:, k], ALU.add).then_inc(merged, 1)
                    if k >= 1:
                        rest_m(k - 1)
                rest_m(KT - 1)
                if not last:
                    rest_y(c + 1)
                for n in range(PT):
                    dve.wait_ge(x_loaded[n], 16 * c + 16)
                    dve.wait_ge(full_out[n], c + 1)
                    dve.tensor_tensor(x_sb[:, n], acc[n][:, :], x_sb[:, n], ALU.add).then_inc(summed[n], 1)
                    dve.wait_ge(squared[n], c + 1)
                    dve.tensor_scalar(mean_sq[:, n:n + 1], sq_sum[:, n:n + 1], 1.0 / D, EPS, ALU.mult,
                                      ALU.add).then_inc(mean_done[n], 1)
                    dve.wait_ge(rms_done[n], c + 1)
                    dve.scalar_tensor_tensor(o_sb[:, n], x_sb[:, n], inv_rms[:, n:n + 1], gain[:, :],
                                             ALU.mult, ALU.mult).then_inc(o_done[n], 1)

            rest_y(0)
            split_weight_pieces(None, dve, w_pieces_, None, w_hi_done, w_lo_done)
            dve.wait_ge(gain_loaded, 16)
            body(0, False)
            with dve.Fori(1, NPW - 1) as c:
                body(c, False)
            body(NPW - 1, True)

        @block.tensor
        def _(pe):
            def body(c):
                first = isinstance(c, int)
                pe.wait_ge(y_lo_done, c + 1)
                for k in range(KT):
                    if first and k % 2 == 0:
                        pe.wait_ge(w_lo_done, k // 2 + 1)
                    if not (first and k < 4):
                        pe.wait_ge(gated, KT * c + (k - 3))
                    out_, ks = p_ps[k % 4][:, 0:PW], slice(k * P, (k + 1) * P)
                    for j in range(KT):
                        pe.matmul(out_, wo_hi[:, j, ks], y_hi[:, j], start=(j == 0), stop=False)
                        pe.matmul(out_, wo_hi[:, j, ks], y_lo[:, j], start=False, stop=False)
                        mm = pe.matmul(out_, wo_lo[:, j, ks], y_hi[:, j], start=False, stop=(j == KT - 1))
                    mm.then_inc(full, 1)
                for n in range(PT):
                    ts = slice(n * P, (n + 1) * P)
                    wait_past(pe, summed[n], c)
                    for half in range(HALVES):
                        cols = slice(half * CW, (half + 1) * CW)
                        for k in range(KT):
                            if (n, half) == (0, 0):
                                pe.wait_ge(m_lo_done, KT * c + (k + 1))
                                if first and k == 0:
                                    pe.wait_ge(w_lo_done, N_PIECES - 2)
                            if first and (n, half, k) == (0, 1, 0):
                                pe.wait_ge(w_lo_done, N_PIECES)
                            pe.matmul(acc[n][:, cols], m_hi[:, k, ts], wf_hi[:, k, cols], start=(k == 0), stop=False)
                            pe.matmul(acc[n][:, cols], m_hi[:, k, ts], wf_lo[:, k, cols], start=False, stop=False)
                            mm = pe.matmul(acc[n][:, cols], m_lo[:, k, ts], wf_hi[:, k, cols], start=False,
                                           stop=(k == KT - 1))
                    mm.then_inc(full_out[n], 1)

            turns_from_first(pe, NPW, body)


def hybrid_block(nc, x, norm_in, w_in, norm_v, w_s, b_s, w_o_gmlp, w_o_sb, w_out, norm_final, out):
    s = {n: nc.dram_tensor(n, [D, S], F32, kind="Internal").ap()
         for n in ("uz_T", "va_T", "q_T", "k_T", "vb_T", "zb_T", "ga_T", "gb_T", "pa_T", "yb_T")}
    norm_and_project(nc, x, norm_in, w_in, s)
    gate_and_project_a(nc, norm_v, w_s, b_s, w_o_gmlp, s)
    attention(nc, s)
    merge_and_project_out(nc, x, w_o_sb, w_out, norm_final, out, s)


_INS = ["x", "norm_in", "w_in", "norm_v", "w_s", "b_s", "w_o_gmlp", "w_o_sb", "w_out", "norm_final"]


def kernel(**inputs):
    import numpy as np
    import concourse.bacc as bacc
    from concourse.bass_utils import run_bass_kernel_spmd

    nc = bacc.Bacc("TRN2", target_bir_lowering=False, num_devices=1)
    arrays, args = {}, []
    for name in _INS:
        a = np.ascontiguousarray(inputs[name])
        arrays[f"in_{name}"] = a
        args.append(nc.dram_tensor(f"in_{name}", a.shape, mybir.dt.from_np(a.dtype), kind="ExternalInput").ap())
    out = nc.dram_tensor("out", [1, S, D], F32, kind="ExternalOutput").ap()
    hybrid_block(nc, *args, out)
    r = run_bass_kernel_spmd(nc, [arrays], core_ids=[0])
    return r.results[0]["out"]
```

```python
from contextlib import ExitStack

import concourse.bass as bass
from concourse import mybir
from concourse.alu_op_type import AluOpType as ALU

ACT = mybir.ActivationFunctionType
F32 = mybir.dt.float32
F32R = mybir.dt.float32r

P = 128
D = 1024
S = 2048
KT = D // P
NT = S // P
CW = 512
NC = S // CW
HEADS = 8
GROUPS = 8
EPS = 1e-6
SCALE = float(P) ** -0.5
MASKED = -1e30
WT = 2 * P
BANKS = 8


class Scope:

    def __init__(self, nc, memory, prefix):
        self.nc, self.memory, self.prefix, self.used = nc, memory, prefix, []

    def clear(self):
        self.nc.clear_and_free_semaphores(self.used)
        self.nc.all_engine_barrier()

    def sb(self, name, shape, dt=F32):
        return self.memory.enter_context(self.nc.sbuf_tensor(f"{self.prefix}_{name}", shape, dt))

    def ps(self, name, shape):
        return self.memory.enter_context(self.nc.psum_tensor(f"{self.prefix}_{name}", shape, F32))

    def sem(self, name):
        self.used.append(self.nc.alloc_semaphore(name=f"{self.prefix}_{name}"))
        return self.used[-1]

    def sems(self, name, n):
        return [self.sem(f"{name}{i}") for i in range(n)]


def wait_past(eng, sem, count):
    if not (isinstance(count, int) and count == 0):
        eng.wait_ge(sem, count)


def turns_from_first(eng, turns, body):
    body(0)
    with eng.Fori(1, turns) as t:
        body(t)


class Projection:

    def __init__(self, sc, act_hi, act_lo, banks):
        self.act_hi, self.act_lo, self.banks = act_hi, act_lo, banks
        self.stage = sc.sb("w_stage", [P, 2, KT, WT])
        self.w_hi = sc.sb("w_hi", [P, 2, KT, WT], F32R)
        self.w_lo = sc.sb("w_lo", [P, 2, KT, WT], F32R)
        self.w_loaded = sc.sems("w_loaded", 2)
        self.hi_split = sc.sems("hi_split", 2)
        self.w_ready = sc.sems("w_ready", 2)
        self.full = [sc.sems(f"full{b}_", BANKS) for b in range(2)]
        self.free = sc.sems("free", BANKS)

    def start(self, reader):
        for i in range(BANKS):
            reader.sem_inc(self.free[i], 1)

    def load(self, sp, turn, b, pieces):
        wait_past(sp, self.w_ready[b], turn)
        for dst, src in pieces:
            sp.dma_start(dst, src).then_inc(self.w_loaded[b], 16)

    def by_rows(self, b, weights, at):
        return [(self.stage[:, b, h * KT // 2:(h + 1) * KT // 2, :],
                 weights[:, h * KT // 2:(h + 1) * KT // 2, bass.ds(at, WT)]) for h in range(2)]

    def split(self, dve, turn, b):
        dve.wait_ge(self.w_loaded[b], 32 * turn + 32)
        wait_past(dve, self.full[b][BANKS - 1], turn)
        dve.tensor_copy(self.w_hi[:, b], self.stage[:, b]).then_inc(self.hi_split[b], 1)
        dve.wait_ge(self.hi_split[b], turn + 1)
        dve.tensor_tensor(self.w_lo[:, b], self.stage[:, b], self.w_hi[:, b].bitcast(F32),
                          ALU.subtract).then_inc(self.w_ready[b], 1)

    def multiply(self, pe, turn, b):
        pe.wait_ge(self.w_ready[b], turn + 1)
        for m in range(2):
            for c in range(NC):
                i = m * NC + c
                out, cols, ws = self.banks[i][:, :], slice(c * CW, (c + 1) * CW), slice(m * P, (m + 1) * P)
                pe.wait_ge(self.free[i], 2 * turn + b + 1)
                for k in range(KT):
                    hi, lo = self.w_hi[:, b, k, ws], self.w_lo[:, b, k, ws]
                    pe.matmul(out, hi, self.act_hi[:, k, cols], start=(k == 0), stop=False)
                    pe.matmul(out, hi, self.act_lo[:, k, cols], start=False, stop=False)
                    mm = pe.matmul(out, lo, self.act_hi[:, k, cols], start=False, stop=(k == KT - 1))
                mm.then_inc(self.full[b][i], 1)


def make_identity(pool, ident, zeroed, done):
    pool.memset(ident[:, :], 0.0).then_inc(zeroed, 1)
    pool.wait_ge(zeroed, 1)
    pool.affine_select(out=ident[:, :], in_=ident[:, :], compare_op=ALU.not_equal, fill=1.0, base=0,
                       pattern=[[-1, P]], channel_multiplier=1).then_inc(done, 1)


def norm_and_project(nc, x, norm_in, w_in, w_o_gmlp, s, carried):
    x_t = x.rearrange("a (t p) d -> (a t) p d", p=P)
    w_k = w_in.rearrange("a (k p) f -> p (a k) f", p=P)
    U, VA, ZA, Q, K, VB, ZB, GA, GB = (i * D for i in range(9))
    single = [(VA, ACT.Gelu_apprx_tanh, s["va_T"]), (Q, ACT.Copy, s["q_T"]), (K, ACT.Copy, s["k_T"]),
              (VB, ACT.Copy, s["vb_T"]), (ZB, ACT.Silu, s["zb_T"]), (GA, ACT.Sigmoid, s["ga_T"]),
              (GB, ACT.Sigmoid, s["gb_T"])]
    UZ = KT // 2
    PER = D // WT // 2
    TURNS = UZ + PER * len(single)

    with ExitStack() as memory:
        sc = Scope(nc, memory, "in")
        h_hi = sc.sb("h_hi", [P, KT, S], F32R)
        h_lo = sc.sb("h_lo", [P, KT, S], F32R)
        banks = [sc.ps(f"bank{i}", [P, CW]) for i in range(BANKS)]
        pj = Projection(sc, h_hi, h_lo, banks)
        o_sb = sc.sb("o_sb", [P, BANKS, CW])
        x_sb = carried.as_tiles(0)
        gain = sc.sb("gain", [P, D])
        ident = sc.sb("ident", [P, P])
        sq_sum = sc.sb("sq_sum", [P, 2])
        mean_sq = sc.sb("mean_sq", [P, 2])
        inv_rms = sc.sb("inv_rms", [P, 2])
        minus_half = sc.sb("minus_half", [P, 1])

        gain_loaded, zeroed, ident_done, half_set = (
            sc.sem(n) for n in ("gain_loaded", "zeroed", "ident_done", "half_set"))
        x_loaded = sc.sems("x_loaded", 2)
        squared = sc.sems("squared", 2)
        mean_done = sc.sems("mean_done", 2)
        rms_done = sc.sems("rms_done", 2)
        scaled = sc.sems("scaled", 2)
        turned = sc.sems("turned", 2)
        hi_done = sc.sems("hi_done", 2)
        lo_done = sc.sems("lo_done", 2)
        multiplied = sc.sems("multiplied", NC)
        stored = sc.sems("stored", BANKS)
        memory.callback(sc.clear)
        block = memory.enter_context(nc.Block())

        @block.sync
        def _(sp):
            sp.dma_start(x_sb[:, 0], x_t[0]).then_inc(x_loaded[0], 16)
            sp.dma_start(x_sb[:, 1], x_t[1]).then_inc(x_loaded[1], 16)
            sp.dma_start(gain[:, :], norm_in[0:1, :].to_broadcast([P, D])).then_inc(gain_loaded, 16)
            for b in range(2):
                pj.load(sp, 0, b, [(pj.stage[:, b, :, 0:P], w_k[:, :, b * P:(b + 1) * P]),
                                   (pj.stage[:, b, :, P:WT], w_k[:, :, ZA + b * P:ZA + (b + 1) * P])])
            with sp.Fori(1, NT // 2) as t:
                for b in range(2):
                    tile = sp.snap(2 * t + b)
                    sp.wait_ge(turned[b], t)
                    sp.dma_start(x_sb[:, b], x_t[bass.ds(tile, 1)].rearrange("a p d -> p (a d)"))\
                        .then_inc(x_loaded[b], 16)
            with sp.Fori(1, UZ) as t:
                for b in range(2):
                    u_at, z_at = sp.snap(U + (2 * t + b) * P), sp.snap(ZA + (2 * t + b) * P)
                    pj.load(sp, t, b, [(pj.stage[:, b, :, 0:P], w_k[:, :, bass.ds(u_at, P)]),
                                       (pj.stage[:, b, :, P:WT], w_k[:, :, bass.ds(z_at, P)])])
            for n, (at, _, _) in enumerate(single):
                with sp.Fori(0, PER) as t:
                    for b in range(2):
                        w_at = sp.snap(at + (2 * t + b) * WT)
                        pj.load(sp, t + (UZ + n * PER), b, pj.by_rows(b, w_k, w_at))
                if n == 0:
                    sp.wait_ge(turned[1], NT // 2)
                    sp.dma_start(carried.as_weights(0), w_piece(w_o_gmlp, 0)).then_inc(carried.wo_a_loaded, 16)

        @block.gpsimd
        def _(pool):
            pool.memset(minus_half[:, :], -0.5).then_inc(half_set, 1)
            make_identity(pool, ident, zeroed, ident_done)
            pool.wait_ge(half_set, 1)
            with pool.Fori(0, NT // 2) as t:
                for b in range(2):
                    pool.wait_ge(mean_done[b], t + 1)
                    pool.tensor_tensor(inv_rms[:, b:b + 1], mean_sq[:, b:b + 1], minus_half[:, :],
                                       ALU.pow).then_inc(rms_done[b], 1)
            with pool.Fori(0, UZ) as t:
                for b in range(2):
                    for c in range(NC):
                        pool.wait_ge(pj.free[c], 2 * t + b + 2)
                        pool.wait_ge(pj.free[NC + c], 2 * t + b + 2)
                        pool.tensor_tensor(o_sb[:, c], o_sb[:, c], o_sb[:, NC + c], ALU.mult)\
                            .then_inc(multiplied[c], 1)

        @block.scalar
        def _(act):
            def sum_squares(t, b):
                act.wait_ge(x_loaded[b], 16 * t + 16)
                act.activation(o_sb[:, 2 * b:2 * b + 2].rearrange("p a c -> p (a c)"), x_sb[:, b], ACT.Square,
                               accum_out=sq_sum[:, b:b + 1]).then_inc(squared[b], 1)

            def round_hi(t, b, at):
                act.wait_ge(turned[b], t + 1)
                for half in range(2):
                    ins = act.activation(h_hi[:, 4 * half:4 * half + 4, bass.ds(at, P)],
                                         banks[2 * b + half][:, :].rearrange("p (k c) -> p k c", k=4), ACT.Copy)
                ins.then_inc(hi_done[b], 1)

            sum_squares(0, 0)
            with act.Fori(0, NT // 2 - 1) as t:
                sum_squares(t, 1)
                round_hi(t, 0, 2 * t * P)
                sum_squares(t + 1, 0)
                round_hi(t, 1, (2 * t + 1) * P)
            last = NT // 2 - 1
            sum_squares(last, 1)
            round_hi(last, 0, 2 * last * P)
            round_hi(last, 1, (2 * last + 1) * P)

            act.wait_ge(squared[1], NT // 2)

            pj.start(act)

            def gelu_silu(t):
                for b in range(2):
                    row = (2 * t + b) * P
                    for c in range(NC):
                        act.wait_ge(pj.full[b][c], t + 1)
                        wait_past(act, stored[c], 16 * (2 * t + b))
                        act.activation(o_sb[:, c], banks[c][:, :], ACT.Gelu_apprx_tanh).then_inc(pj.free[c], 1)
                    for c in range(NC):
                        i = NC + c
                        act.wait_ge(pj.full[b][i], t + 1)
                        wait_past(act, multiplied[c], 2 * t + b)
                        act.activation(o_sb[:, i], banks[i][:, :], ACT.Silu).then_inc(pj.free[i], 1)
                    for c in range(NC):
                        act.wait_ge(multiplied[c], 2 * t + b + 1)
                        act.dma_start(s["uz_T"][bass.ds(row, P), c * CW:(c + 1) * CW], o_sb[:, c])\
                            .then_inc(stored[c], 16)

            turns_from_first(act, UZ, gelu_silu)
            for n, (_, func, dst) in enumerate(single):
                before = UZ + n * PER

                def one_output(t):
                    for b in range(2):
                        for i in range(BANKS):
                            m, c = divmod(i, NC)
                            row = ((2 * t + b) * 2 + m) * P
                            step = 2 * (t + before) + b
                            act.wait_ge(pj.full[b][i], t + (before + 1))
                            wait_past(act, stored[i], 16 * (step - (0 if i < NC else 2 * UZ)))
                            act.activation(o_sb[:, i], banks[i][:, :], func).then_inc(pj.free[i], 1)
                            act.wait_ge(pj.free[i], step + 2)
                            act.dma_start(dst[bass.ds(row, P), c * CW:(c + 1) * CW], o_sb[:, i])\
                                .then_inc(stored[i], 16)

                if n == 0:
                    turns_from_first(act, PER, one_output)
                else:
                    with act.Fori(0, PER) as t:
                        one_output(t)
            for i in range(BANKS):
                act.wait_ge(stored[i], 16 * 2 * (TURNS if i < NC else TURNS - UZ))

        @block.vector
        def _(dve):
            def mean(t, b):
                dve.wait_ge(squared[b], t + 1)
                dve.tensor_scalar(mean_sq[:, b:b + 1], sq_sum[:, b:b + 1], 1.0 / D, EPS, ALU.mult, ALU.add)\
                    .then_inc(mean_done[b], 1)

            def scale(t, b):
                dve.wait_ge(rms_done[b], t + 1)
                dve.scalar_tensor_tensor(x_sb[:, b], x_sb[:, b], inv_rms[:, b:b + 1], gain[:, :], ALU.mult,
                                         ALU.mult).then_inc(scaled[b], 1)

            def rest_lo(t, b, at):
                dve.wait_ge(hi_done[b], t + 1)
                for half in range(2):
                    ks = slice(4 * half, 4 * half + 4)
                    ins = dve.tensor_tensor(h_lo[:, ks, bass.ds(at, P)],
                                            banks[2 * b + half][:, :].rearrange("p (k c) -> p k c", k=4),
                                            h_hi[:, ks, bass.ds(at, P)].bitcast(F32), ALU.subtract)
                ins.then_inc(lo_done[b], 1)

            for b in range(2):
                dve.sem_inc(lo_done[b], 1)
            dve.wait_ge(gain_loaded, 16)
            mean(0, 0)
            scale(0, 0)
            with dve.Fori(0, NT // 2 - 1) as t:
                mean(t, 1)
                scale(t, 1)
                rest_lo(t, 0, 2 * t * P)
                mean(t + 1, 0)
                scale(t + 1, 0)
                rest_lo(t, 1, (2 * t + 1) * P)
            last = NT // 2 - 1
            mean(last, 1)
            scale(last, 1)
            rest_lo(last, 0, 2 * last * P)
            rest_lo(last, 1, (2 * last + 1) * P)

            def split(t):
                for b in range(2):
                    pj.split(dve, t, b)

            turns_from_first(dve, TURNS, split)

        @block.tensor
        def _(pe):
            pe.wait_ge(ident_done, 1)
            with pe.Fori(0, NT // 2) as t:
                for b in range(2):
                    pe.wait_ge(scaled[b], t + 1)
                    pe.wait_ge(lo_done[b], t + 1)
                    for k in range(KT):
                        ins = pe.transpose(banks[2 * b + k // 4][:, (k % 4) * P:(k % 4 + 1) * P],
                                           x_sb[:, b, k * P:(k + 1) * P], ident[:, :])
                    ins.then_inc(turned[b], 1)
            for b in range(2):
                pe.wait_ge(lo_done[b], NT // 2 + 1)
            with pe.Fori(0, TURNS) as t:
                for b in range(2):
                    pj.multiply(pe, t, b)


N_CARRIED = 3
PW = 2 * P
PT = PW // P
NPW = S // PW


def w_piece(w, n):
    return w.rearrange("a (k p) f -> p (a k) f", p=P)[:, :, n * WT:(n + 1) * WT]


def round_weights(act, pieces, n, hi_done):
    stage, hi, _, loaded, count = pieces[n]
    act.wait_ge(loaded, count)
    act.activation(hi, stage, ACT.Copy).then_inc(hi_done, 1)


def rest_weights(dve, pieces, n, hi_done, lo_done):
    stage, hi, lo, _, _ = pieces[n]
    dve.wait_ge(hi_done, n + 1)
    dve.tensor_tensor(lo, stage, hi.bitcast(F32), ALU.subtract).then_inc(lo_done, 1)


def gate_and_project_a(nc, norm_v, w_s, b_s, w_o_gmlp, s, carried):
    va_n = s["va_T"].rearrange("(g c) s -> c g s", c=P)
    uz_n = s["uz_T"].rearrange("(g c) s -> c g s", c=P)
    ga_k = s["ga_T"].rearrange("(k p) s -> p k s", p=P)
    pa_k = s["pa_T"].rearrange("(k p) s -> p k s", p=P)
    with ExitStack() as memory:
        sc = Scope(nc, memory, "a")
        ident = sc.sb("ident", [P, P])
        w_sb = sc.sb("w_sb", [P, GROUPS, P])
        wT_hi = sc.sb("wT_hi", [P, GROUPS, P], F32R)
        wT_lo = sc.sb("wT_lo", [P, GROUPS, P], F32R)
        bias = sc.sb("bias", [P, GROUPS, P])
        gain = sc.sb("gain", [P, GROUPS])
        va = sc.sb("va", [P, 2, GROUPS, P])
        uz = sc.sb("uz", [P, 2, GROUPS, P])
        v_hi = sc.sb("v_hi", [P, 2, D], F32R)
        v_lo = sc.sb("v_lo", [P, 2, D], F32R)
        y = sc.sb("y", [P, 2, GROUPS, P])
        squares = sc.sb("squares", [P, D])
        sq_sum, mean_sq, inv_rms = (sc.sb(n, [P, 2]) for n in ("sq_sum", "mean_sq", "inv_rms"))
        minus_half = sc.sb("minus_half", [P, 1])
        ya_hi = sc.sb("ya_hi", [P, 2, KT, PW], F32R)
        ya_lo = sc.sb("ya_lo", [P, 2, KT, PW], F32R)
        gate = sc.sb("gate", [P, 2, KT, PW])
        wo_hi = sc.sb("wo_hi", [P, KT, D], F32R)
        wo_lo = sc.sb("wo_lo", [P, KT, D], F32R)
        v_ps = sc.ps("v_ps", [P, D])
        m_ps = sc.ps("m_ps", [P, D])
        p_ps = [sc.ps(f"p_ps{n}", [P, CW]) for n in range(4)]

        w_loaded, bias_loaded, gain_loaded, zeroed, ident_done, half_set, masked, w_turned, w_hi_done, w_done = (
            sc.sem(n) for n in ("w_loaded", "bias_loaded", "gain_loaded", "zeroed", "ident_done", "half_set",
                                "masked", "w_turned", "w_hi_done", "w_done"))
        wo_loaded = sc.sem("wo_loaded")
        wo_hi_done, wo_lo_done = sc.sem("wo_hi_done"), sc.sem("wo_lo_done")
        turned, squared, mean_done, rms_done, v_hi_done, v_lo_done, mixed, gained, biased, y_done, y_hi_done, \
            y_lo_done = (sc.sem(n) for n in (
                "turned", "squared", "mean_done", "rms_done", "v_hi_done", "v_lo_done", "mixed", "gained",
                "biased", "y_done", "y_hi_done", "y_lo_done"))
        va_loaded, uz_loaded, gate_loaded, stored = (
            sc.sems(n, 2) for n in ("va_loaded", "uz_loaded", "gate_loaded", "stored"))
        full, gated = sc.sem("full"), sc.sem("gated")
        block = memory.enter_context(nc.Block())

        def per_two_chunks(eng, body):
            body(0, False)
            with eng.Fori(1, NPW // 2 - 1) as t:
                body(t, False)
            body(NPW // 2 - 1, True)

        N_WO = D // WT
        wo_pieces = [(carried.as_weights(n % 3), wo_hi[:, :, n * WT:(n + 1) * WT], wo_lo[:, :, n * WT:(n + 1) * WT],
                      *((wo_loaded, 16 * n) if n else (carried.wo_a_loaded, 16))) for n in range(N_WO)]

        @block.sync
        def _(sp):
            def load_tile(tile, b, at):
                first = isinstance(tile, int) and tile < 2
                if not first:
                    sp.wait_ge(turned, tile - 1)
                sp.dma_start(va[:, b], va_n[:, :, bass.ds(at, P)]).then_inc(va_loaded[b], 16)
                if not first:
                    sp.wait_ge(y_done, tile - 1)
                sp.dma_start(uz[:, b], uz_n[:, :, bass.ds(at, P)]).then_inc(uz_loaded[b], 16)

            def snap(x):
                return x if isinstance(x, int) else sp.snap(x)

            def load_wo(n):
                if n >= 2:
                    sp.wait_ge(wo_loaded, 16 * (n - 1))
                if n >= 3:
                    sp.wait_ge(wo_lo_done, n - 2)
                sp.dma_start(wo_pieces[n][0], w_piece(w_o_gmlp, n)).then_inc(wo_loaded, 16)

            sp.dma_start(va[:, 0], va_n[:, :, 0:P]).then_inc(va_loaded[0], 16)
            sp.dma_start(w_sb[:, :, :], w_s[0].rearrange("g t s -> t g s")).then_inc(w_loaded, 16)
            sp.dma_start(va[:, 1], va_n[:, :, P:2 * P]).then_inc(va_loaded[1], 16)
            with nc.allow_non_contiguous_dma(reason="1024 gains, one to a partition"):
                sp.dma_start(gain[:, :], norm_v[0].rearrange("(g c) -> c g", c=P)).then_inc(gain_loaded, 16)
            sp.dma_start(bias[:, :, :].rearrange("p g t -> p (g t)"),
                         b_s.rearrange("a g t -> a (g t)").to_broadcast([P, D])).then_inc(bias_loaded, 16)
            sp.dma_start(uz[:, 0], uz_n[:, :, 0:P]).then_inc(uz_loaded[0], 16)
            sp.dma_start(uz[:, 1], uz_n[:, :, P:2 * P]).then_inc(uz_loaded[1], 16)
            for n in range(1, N_WO):
                load_wo(n)

            def body(t, last):
                for b in range(2):
                    at = snap((2 * t + b) * PW)
                    ats = [snap((2 * t + b + 1) * PW + n * P) for n in range(PT)]
                    wait_past(sp, stored[b], 16 * t)
                    sp.dma_start(gate[:, b], ga_k[:, :, bass.ds(at, PW)]).then_inc(gate_loaded[b], 16)
                    if not (last and b == 1):
                        for n in range(PT):
                            load_tile(PT * (2 * t + b + 1) + n, n, ats[n])

            per_two_chunks(sp, body)
            sp.wait_ge(wo_lo_done, N_WO)
            for n, name in enumerate(("q_T", "k_T")):
                sp.dma_start(carried.buffer[n][:, :], s[name][0:P, :]).then_inc(carried.q_k_loaded, 16)
            sp.dma_start(carried.buffer[2][:, :], s["vb_T"][0:P, :]).then_inc(carried.v_loaded, 16)

        @block.gpsimd
        def _(pool):
            pool.memset(minus_half[:, :], -0.5).then_inc(half_set, 1)
            make_identity(pool, ident, zeroed, ident_done)
            pool.wait_ge(w_loaded, 16)
            pool.affine_select(out=w_sb[:, :, :], in_=w_sb[:, :, :], compare_op=ALU.is_ge, fill=0.0, base=0,
                               pattern=[[0, GROUPS], [-1, P]], channel_multiplier=1).then_inc(masked, 1)
            pool.wait_ge(half_set, 1)
            pool.wait_ge(bias_loaded, 16)

            def rms(tile, b):
                pool.wait_ge(mean_done, tile + 1)
                pool.tensor_tensor(inv_rms[:, b:b + 1], mean_sq[:, b:b + 1], minus_half[:, :],
                                   ALU.pow).then_inc(rms_done, 1)

            def add_bias(tile, b):
                pool.wait_ge(gained, tile + 1)
                pool.tensor_tensor(y[:, b], y[:, b], bias[:, :, :], ALU.add).then_inc(biased, 1)

            rms(0, 0)
            rms(1, 1)
            add_bias(0, 0)
            add_bias(1, 1)
            with pool.Fori(1, NT // 2) as t:
                for b in range(2):
                    rms(2 * t + b, b)
                    add_bias(2 * t + b, b)

        @block.scalar
        def _(act):
            def sum_squares(tile, b):
                act.wait_ge(turned, tile + 1)
                act.activation(squares[:, :], v_ps[:, :], ACT.Square,
                               accum_out=sq_sum[:, b:b + 1]).then_inc(squared, 1)

            def round_v(tile, b):
                act.wait_ge(rms_done, tile + 1)
                if not isinstance(tile, int) or tile >= 2:
                    act.wait_ge(mixed, tile - 1)
                act.activation(v_hi[:, b], v_ps[:, :], ACT.Copy, scale=inv_rms[:, b:b + 1])\
                    .then_inc(v_hi_done, 1)

            def round_y(tile, b, chunk, cb):
                act.wait_ge(y_done, tile + 1)
                if not isinstance(chunk, int) or chunk >= 2:
                    act.wait_ge(full, KT * chunk - KT)
                act.activation(ya_hi[:, cb, :, b * P:(b + 1) * P], y[:, b], ACT.Copy).then_inc(y_hi_done, 1)

            act.wait_ge(w_turned, 1)
            act.activation(wT_hi[:, :, :].rearrange("p g t -> p (g t)"), m_ps[:, :], ACT.Copy).then_inc(w_hi_done, 1)
            sum_squares(0, 0)
            round_v(0, 0)
            round_weights(act, wo_pieces, 0, wo_hi_done)
            sum_squares(1, 1)
            round_v(1, 1)
            round_y(0, 0, 0, 0)
            round_weights(act, wo_pieces, 1, wo_hi_done)
            round_y(1, 1, 0, 0)
            for n in range(2, N_WO):
                round_weights(act, wo_pieces, n, wo_hi_done)

            def body(t, last):
                for b in range(2):
                    chunk = 2 * t + b
                    if not (last and b == 1):
                        nxt = PT * (chunk + 1)
                        sum_squares(nxt, 0)
                        round_v(nxt, 0)
                        sum_squares(nxt + 1, 1)
                        round_y(nxt, 0, chunk + 1, 1 - b)
                        round_v(nxt + 1, 1)
                        round_y(nxt + 1, 1, chunk + 1, 1 - b)
                    at = chunk * PW
                    act.wait_ge(gated, KT * chunk + KT)
                    act.dma_start(pa_k[:, :, bass.ds(at, PW)], gate[:, b]).then_inc(stored[b], 16)

            per_two_chunks(act, body)
            for b in range(2):
                act.wait_ge(stored[b], 16 * (NPW // 2))

        @block.vector
        def _(dve):
            def mean(tile, b):
                dve.wait_ge(squared, tile + 1)
                dve.tensor_scalar(mean_sq[:, b:b + 1], sq_sum[:, b:b + 1], 1.0 / D, EPS, ALU.mult,
                                  ALU.add).then_inc(mean_done, 1)

            def rest_v(tile, b):
                dve.wait_ge(v_hi_done, tile + 1)
                dve.scalar_tensor_tensor(v_lo[:, b], v_ps[:, :], inv_rms[:, b:b + 1],
                                         v_hi[:, b].bitcast(F32), ALU.mult, ALU.subtract).then_inc(v_lo_done, 1)

            def gain_mix(tile, b):
                dve.wait_ge(mixed, tile + 1)
                dve.tensor_tensor(y[:, b], m_ps[:, :].rearrange("p (g t) -> p g t", g=GROUPS),
                                  gain[:, :].unsqueeze(2).to_broadcast([P, GROUPS, P]), ALU.mult)\
                    .then_inc(gained, 1)

            def times_uz(tile, b, loads):
                dve.wait_ge(biased, tile + 1)
                dve.wait_ge(uz_loaded[b], 16 * loads)
                dve.tensor_tensor(y[:, b], y[:, b], uz[:, b], ALU.mult).then_inc(y_done, 1)

            def rest_y(tile, b, cb):
                dve.wait_ge(y_hi_done, tile + 1)
                dve.tensor_tensor(ya_lo[:, cb, :, b * P:(b + 1) * P], y[:, b],
                                  ya_hi[:, cb, :, b * P:(b + 1) * P].bitcast(F32), ALU.subtract)\
                    .then_inc(y_lo_done, 1)

            dve.wait_ge(w_hi_done, 1)
            dve.tensor_tensor(wT_lo[:, :, :].rearrange("p g t -> p (g t)"), m_ps[:, :],
                              wT_hi[:, :, :].rearrange("p g t -> p (g t)").bitcast(F32), ALU.subtract)\
                .then_inc(w_done, 1)
            dve.wait_ge(gain_loaded, 16)
            mean(0, 0)
            rest_v(0, 0)
            rest_weights(dve, wo_pieces, 0, wo_hi_done, wo_lo_done)
            mean(1, 1)
            rest_v(1, 1)
            gain_mix(0, 0)
            times_uz(0, 0, 1)
            rest_y(0, 0, 0)
            gain_mix(1, 1)
            rest_weights(dve, wo_pieces, 1, wo_hi_done, wo_lo_done)
            times_uz(1, 1, 1)
            rest_y(1, 1, 0)
            for n in range(2, N_WO):
                rest_weights(dve, wo_pieces, n, wo_hi_done, wo_lo_done)

            def body(t, last):
                for b in range(2):
                    chunk = 2 * t + b

                    def apply_gate(k):
                        if k == 0:
                            dve.wait_ge(gate_loaded[b], 16 * t + 16)
                        dve.wait_ge(full, KT * chunk + (k + 1))
                        dve.tensor_tensor(gate[:, b, k], p_ps[k % 4][:, 0:PW], gate[:, b, k], ALU.mult)\
                            .then_inc(gated, 1)

                    if last and b == 1:
                        for k in range(KT):
                            apply_gate(k)
                        continue
                    nxt, cb = PT * (chunk + 1), 1 - b
                    mean(nxt, 0)
                    apply_gate(0)
                    rest_v(nxt, 0)
                    apply_gate(1)
                    gain_mix(nxt, 0)
                    apply_gate(2)
                    times_uz(nxt, 0, chunk + 2)
                    mean(nxt + 1, 1)
                    apply_gate(3)
                    rest_y(nxt, 0, cb)
                    rest_v(nxt + 1, 1)
                    apply_gate(4)
                    gain_mix(nxt + 1, 1)
                    apply_gate(5)
                    times_uz(nxt + 1, 1, chunk + 2)
                    apply_gate(6)
                    rest_y(nxt + 1, 1, cb)
                    apply_gate(7)

            per_two_chunks(dve, body)

        @block.tensor
        def _(pe):
            def turn(tile, b, loads):
                pe.wait_ge(va_loaded[b], 16 * loads)
                wait_past(pe, v_lo_done, tile)
                for g in range(GROUPS):
                    ins = pe.transpose(v_ps[:, g * P:(g + 1) * P], va[:, b, g, :], ident[:, :])
                ins.then_inc(turned, 1)

            def mix(tile, b):
                pe.wait_ge(v_lo_done, tile + 1)
                wait_past(pe, gained, tile)
                for g in range(GROUPS):
                    gs = slice(g * P, (g + 1) * P)
                    pe.matmul(m_ps[:, gs], v_hi[:, b, gs], wT_hi[:, g], start=True, stop=False)
                    pe.matmul(m_ps[:, gs], v_hi[:, b, gs], wT_lo[:, g], start=False, stop=False)
                    mm = pe.matmul(m_ps[:, gs], v_lo[:, b, gs], wT_hi[:, g], start=False, stop=True)
                mm.then_inc(mixed, 1)

            pe.wait_ge(ident_done, 1)
            pe.wait_ge(masked, 1)
            for g in range(GROUPS):
                ins = pe.transpose(m_ps[:, g * P:(g + 1) * P], w_sb[:, g, :], ident[:, :])
            ins.then_inc(w_turned, 1)
            turn(0, 0, 1)
            pe.wait_ge(w_done, 1)
            turn(1, 1, 1)
            mix(0, 0)
            mix(1, 1)

            def body(t, last):
                for b in range(2):
                    chunk = 2 * t + b

                    def project(k):
                        if k == 0:
                            pe.wait_ge(y_lo_done, PT * chunk + PT)
                        if isinstance(chunk, int) and chunk == 0 and k % 2 == 0:
                            pe.wait_ge(wo_lo_done, k // 2 + 1)
                        if not (isinstance(chunk, int) and chunk == 0 and k < 4):
                            pe.wait_ge(gated, KT * chunk + (k - 3))
                        out, ks = p_ps[k % 4][:, 0:PW], slice(k * P, (k + 1) * P)
                        for j in range(KT):
                            pe.matmul(out, wo_hi[:, j, ks], ya_hi[:, b, j], start=(j == 0), stop=False)
                            pe.matmul(out, wo_hi[:, j, ks], ya_lo[:, b, j], start=False, stop=False)
                            mm = pe.matmul(out, wo_lo[:, j, ks], ya_hi[:, b, j], start=False, stop=(j == KT - 1))
                        mm.then_inc(full, 1)

                    nxt = PT * (chunk + 1)
                    mixes = {} if last and b == 1 else {
                        0: lambda: turn(nxt, 0, chunk + 2), 2: lambda: mix(nxt, 0),
                        3: lambda: turn(nxt + 1, 1, chunk + 2), 5: lambda: mix(nxt + 1, 1)}
                    for k in range(KT):
                        if k in mixes:
                            mixes[k]()
                        project(k)

            per_two_chunks(pe, body)


QT = CW // P
NSUP = NT // QT
ZW = CW
Z_BANKS = 3
Y_BANKS = 2
AHEAD = 3
T_BANKS = 3
W_LAG = 0
QK_WEIGHT, QK_REST = 1, 3
SPLIT_PLACES = (4, 8, 12), (1, 2, 3, 5)
SPLITS = [("q", 0), ("q", 1), ("q", 2), ("k", 0), ("k", 1), ("q", 3), ("k", 2), ("k", 3)]
EARLY_SPLITS = 3


def blend(some, others):
    def spread(which, events):
        total, so_far = sum(w for _, w in events), 0
        for e, w in events:
            yield (so_far + w / 2) / total, which, e
            so_far += w

    return [e for _, _, e in sorted([*spread(0, some), *spread(1, others)], key=lambda a: a[:2])]


def z_pieces(sup):
    return [("Z", i, at, min(ZW, (i + 1) * P - at)) for i in range(sup * QT, (sup + 1) * QT)
            for at in reversed(range(0, (i + 1) * P, ZW))]


def b_steps(sup):
    wide, narrow = list(range(1, QT * sup + 1)), list(reversed(range(QT * sup + 1, QT * (sup + 1))))
    order = [0]
    while wide or narrow:
        order += [tiles.pop(0) for tiles in (narrow, wide) if tiles]
    return [("B", sup, kt) for kt in order]


def with_splits(logits, splits, at):
    out = list(logits)
    for split, place in reversed(list(zip(splits, at))):
        out.insert(place, split)
    return out


def head_order(last):
    products = [(("V", g), 1) for g in range(NT // QT)]
    products += [(e, min(QT, QT * (e[1] + 1) - e[2])) for sup in range(NSUP) for e in b_steps(sup)]
    def logits(*sups):
        return [(e, e[3] // P) for sup in sups for e in z_pieces(sup)]

    def splits(first, last):
        return [(("QK", part), QK_WEIGHT) for part in range(first, last)]

    if not last:
        ahead = with_splits(logits(NSUP - 1), splits(0, EARLY_SPLITS), SPLIT_PLACES[0])
        ahead += splits(EARLY_SPLITS, EARLY_SPLITS + 1) + [(None, QK_REST)]
        ahead += with_splits(logits(*range(NSUP - 1)), splits(EARLY_SPLITS + 1, len(SPLITS)), SPLIT_PLACES[1])
    else:
        ahead = logits(NSUP - 1) + [(None, len(SPLITS) * QK_WEIGHT + QK_REST +
                                     sum(w for _, w in logits(*range(NSUP - 1))))]
    order, pending = [], []
    for e in blend(ahead, products):
        kind = None if e is None else e[0]
        if kind == "Z":
            order.append(e)
            pending.append(("W", *e[1:]))
            if len(pending) > W_LAG:
                order.append(pending.pop(0))
            continue
        if kind in (None, "QK") or e[:2] == ("B", NSUP - 1):
            order += pending
            pending = []
        if kind is not None:
            order.append(e)
    order += pending
    out, waiting = [], []

    def product():
        _, sup, kt = waiting.pop(0)
        out.append(("P", sup, kt))
        if ("B", sup, kt) == b_steps(sup)[-1]:
            out.append(("Y", sup))

    for e in order:
        out.append(e)
        if e[0] == "B":
            waiting.append(e)
            if len(waiting) > AHEAD:
                product()
    while waiting:
        product()
    return out


def places(order):
    seen = dict.fromkeys("ZWTP", 0)
    for e in order:
        kind = {"V": "T", "B": "T"}.get(e[0], e[0])
        yield e, seen.get(kind)
        if kind in seen:
            seen[kind] += 1


def attention(nc, w_o_sb, s, carried):
    PIECES = sum(len(z_pieces(n)) for n in range(NSUP))
    PRODUCTS = sum(len(b_steps(n)) for n in range(NSUP))
    STEPS = NT // QT + PRODUCTS
    FIRST = sum(len(z_pieces(n)) for n in range(NSUP - 1))
    W_BUFS = 4
    RESTS = 4
    assert PRODUCTS % W_BUFS == 0

    with ExitStack() as memory:
        sc = Scope(nc, memory, "att")
        ident = sc.sb("ident", [P, P])
        ident_r = sc.sb("ident_r", [P, P], F32R)
        mask = sc.sb("mask", [P, P])
        mask_r = sc.sb("mask_r", [P, P], F32R)
        q_in, k_in, v_in = carried.buffer
        q_hi, q_lo, k_hi, k_lo = (sc.sb(n, [P, S], F32R) for n in ("q_hi", "q_lo", "k_hi", "k_lo"))
        v_hi, v_lo = (sc.sb(n, [P, S], F32R) for n in ("v_hi", "v_lo"))
        slot = [sc.sb(f"slot{n}", [P, (n + 1) * P]) for n in range(NT)]
        rest = [sc.sb(f"rest{n}", [P, S + 1]) for n in range(RESTS)]
        wT_hi = [sc.sb(f"wT_hi{n}", [P, CW], F32R) for n in range(W_BUFS)]
        wT_lo = [sc.sb(f"wT_lo{n}", [P, CW], F32R) for n in range(W_BUFS)]
        zb = [sc.sb(f"zb{n}", [P, CW]) for n in range(2)]
        y = [sc.sb(f"y{n}", [P, CW]) for n in range(2)]
        z_ps = [sc.ps(f"z_ps{n}", [P, ZW]) for n in range(Z_BANKS)]
        t_ps = [sc.ps(f"t_ps{n}", [P, CW]) for n in range(T_BANKS)]
        y_ps = [sc.ps(f"y_ps{n}", [P, CW]) for n in range(Y_BANKS)]

        zeroed, ident_done, mask_zeroed, mask_done, consts, ones_set = (
            sc.sem(n) for n in ("zeroed", "ident_done", "mask_zeroed", "mask_done", "consts", "ones_set"))
        qk_loaded, v_loaded = carried.q_k_loaded, carried.v_loaded
        qk_hi, qk_done = sc.sem("qk_hi"), sc.sem("qk_done")
        z_full = sc.sem("z_full")
        z_read = sc.sem("z_read")
        scanned = sc.sem("scanned")
        weighted = sc.sem("weighted")
        turned = sc.sem("turned")
        hi_copied, lo_copied = sc.sem("hi_copied"), sc.sem("lo_copied")
        product = sc.sem("product")
        zb_loaded, y_done, stored = (sc.sems(n, 2) for n in ("zb_loaded", "y_done", "stored"))
        block = memory.enter_context(nc.Block())

        kinds = [e for e, _ in places(head_order(False)) if e[0] in "VB"]

        def t_bank(t):
            return t_ps[t % T_BANKS]

        def last_user(n, a_head, buffers):
            return max(m for m in range(-a_head, n) if m % a_head % buffers == n % buffers)

        def copied(eng, h, t):
            if t >= 0 or not first_head(h):
                eng.wait_ge(lo_copied, STEPS * h + (t + 1))

        def product_of(e):
            return [k for k in kinds if k[0] == "B"].index(e)

        def buffer_free(eng, h, k):
            if not isinstance(h, int) or PRODUCTS * h + k >= W_BUFS:
                eng.wait_ge(product, PRODUCTS * h + (k - W_BUFS + 1))

        def steps_until(sup):
            return max(n + 1 for n, e in enumerate(kinds) if e[:2] == ("B", sup))

        V_READ = max(n + 1 for n, e in enumerate(kinds) if e[0] == "V")
        ALL = [e for n in range(NSUP) for e in z_pieces(n)]

        early = ALL[:FIRST]

        def pieces_before(i):
            return sum(e[1] < i for e in ALL)

        def quarter(part):
            which, n = SPLITS[part]
            return ((q_in, q_hi, q_lo) if which == "q" else (k_in, k_hi, k_lo)), slice(n * CW, (n + 1) * CW)

        def splits_for(sup):
            return max(SPLITS.index((which, n)) + 1 for which in "qk" for n in range(sup + 1))

        def first_head(h):
            return isinstance(h, int) and h == 0

        def products_until(sup):
            return sum(len(b_steps(n)) for n in range(sup + 1))

        def per_head(eng, body):
            body(0, False)
            with eng.Fori(1, HEADS - 1) as h:
                body(h, False)
            body(HEADS - 1, True)

        @block.sync
        def _(sp):
            def load_qk(h):
                row = h * P if isinstance(h, int) else sp.snap(h * P)
                if not isinstance(h, int) or h > 0:
                    sp.wait_ge(qk_done, len(SPLITS) * h)
                sp.dma_start(q_in[:, :], s["q_T"][bass.ds(row, P), :]).then_inc(qk_loaded, 16)
                sp.dma_start(k_in[:, :], s["k_T"][bass.ds(row, P), :]).then_inc(qk_loaded, 16)

            def body(h, last):
                row = h * P if isinstance(h, int) else sp.snap(h * P)
                nxt = (h + 1) * P if isinstance(h, int) else sp.snap((h + 1) * P)
                if not last:
                    load_qk(h + 1)
                if not first_head(h):
                    store_last(h - 1)
                for sup in range(NSUP):
                    n = sup % 2
                    cols = slice(sup * CW, (sup + 1) * CW)
                    wait_past(sp, y_done[n], 2 * h + sup // 2)
                    sp.dma_start(zb[n][:, :], s["zb_T"][bass.ds(row, P), cols]).then_inc(zb_loaded[n], 16)
                    if sup >= 1:
                        m = (sup - 1) % 2
                        sp.wait_ge(y_done[m], 2 * h + ((sup - 1) // 2 + 1))
                        sp.dma_start(s["yb_T"][bass.ds(row, P), (sup - 1) * CW:sup * CW], y[m][:, :])\
                            .then_inc(stored[m], 16)
                    if sup == 0 and not last:
                        sp.wait_ge(turned, STEPS * h + V_READ)
                        sp.dma_start(v_in[:, :], s["vb_T"][bass.ds(nxt, P), :]).then_inc(v_loaded, 16)
                    if sup == 0 and last:
                        sp.wait_ge(qk_done, len(SPLITS) * HEADS)
                        sp.wait_ge(turned, STEPS * h + V_READ)
                        for n in range(N_CARRIED):
                            sp.dma_start(carried.as_weights(n), w_piece(w_o_sb, n)).then_inc(carried.wo_b_loaded, 16)

            def store_last(h):
                row = h * P if isinstance(h, int) else sp.snap(h * P)
                sp.wait_ge(y_done[1], 2 * h + 2)
                sp.dma_start(s["yb_T"][bass.ds(row, P), (NSUP - 1) * CW:], y[1][:, :]).then_inc(stored[1], 16)

            per_head(sp, body)
            store_last(HEADS - 1)
            for n in range(2):
                sp.wait_ge(stored[n], 16 * 2 * HEADS)

        @block.gpsimd
        def _(pool):
            make_identity(pool, ident, zeroed, ident_done)
            pool.memset(mask[:, :], 0.0).then_inc(mask_zeroed, 1)
            pool.wait_ge(mask_zeroed, 1)
            pool.affine_select(out=mask[:, :], in_=mask[:, :], compare_op=ALU.is_gt, fill=MASKED, base=0,
                               pattern=[[-1, P]], channel_multiplier=1).then_inc(mask_done, 1)

            def weights(i, at, width, h, n):
                left = S - (i + 1) * P + at
                a, r = slot[i][:, at:at + width], rest[i % RESTS]
                pool.wait_ge(scanned, PIECES * h + (n + 1))
                pool.tensor_tensor(a, a, r[:, left + 1:left + width + 1], ALU.mult).then_inc(weighted, 1)

            def body(h, last):
                for e, n in places(head_order(last)):
                    if e[0] == "W" and e[1] >= NT - QT:
                        weights(*e[1:], h, FIRST + n)
                    elif e[0] == "W":
                        weights(*e[1:], h + 1, FIRST + n - PIECES)

            for n, e in enumerate(early):
                weights(*e[1:], 0, n)
            per_head(pool, body)

        @block.scalar
        def _(act):
            def split_qk(h, part):
                if part == 0:
                    act.wait_ge(qk_loaded, 32 * h + 32)
                    if not first_head(h):
                        act.wait_ge(z_full, PIECES * h - (PIECES - FIRST))
                if part == EARLY_SPLITS:
                    wait_past(act, z_full, PIECES * h)
                (src, hi, _), cols = quarter(part)
                act.activation(hi[:, cols], src[:, cols], ACT.Copy).then_inc(qk_hi, 1)

            def sigmoids(i, at, width, h, n):
                src = z_ps[n % Z_BANKS][:, 0:width]
                w = (i + 1) * P
                right = S - w + at
                act.wait_ge(z_full, PIECES * h + (n + 1))
                if at + width == w:
                    if not first_head(h):
                        act.wait_ge(turned, STEPS * h + (steps_until(i // QT) - STEPS))
                act.activation(slot[i][:, at:at + width], src, ACT.Sigmoid, scale=SCALE)
                if at + width == w:
                    if i >= RESTS:
                        act.wait_ge(weighted, PIECES * h + pieces_before(i - RESTS + 1))
                    elif not first_head(h):
                        act.wait_ge(weighted, PIECES * h + (pieces_before(NT + i - RESTS + 1) - PIECES))
                act.activation(rest[i % RESTS][:, right:right + width], src, ACT.Sigmoid, scale=-SCALE)\
                    .then_inc(z_read, 1)

            def body(h, last):
                for e, n in places(head_order(last)):
                    if e[0] == "Z" and e[1] >= NT - QT:
                        sigmoids(*e[1:], h, FIRST + n)
                    elif e[0] == "Z":
                        sigmoids(*e[1:], h + 1, FIRST + n - PIECES)
                    elif e[0] == "QK":
                        split_qk(h + 1, e[1])
                    elif e[0] in "VB":
                        copy_hi(h, e, n)

            def copy_hi(h, e, t):
                act.wait_ge(turned, STEPS * h + (t + 1))
                if e[0] == "V":
                    wait_past(act, product, PRODUCTS * h)
                    act.activation(v_hi[:, e[1] * CW:(e[1] + 1) * CW], t_bank(t)[:, :],
                                   ACT.Copy).then_inc(hi_copied, 1)
                else:
                    k, c0 = product_of(e), max(0, e[2] - QT * e[1]) * P
                    buffer_free(act, h, k)
                    act.activation(wT_hi[k % W_BUFS][:, c0:], t_bank(t)[:, c0:], ACT.Copy).then_inc(hi_copied, 1)

            for part in range(len(SPLITS)):
                split_qk(0, part)
            act.wait_ge(ones_set, RESTS)
            for n, e in enumerate(early):
                sigmoids(*e[1:], 0, n)
            per_head(act, body)

        @block.vector
        def _(dve):
            def split_qk(h, part):
                dve.wait_ge(qk_hi, len(SPLITS) * h + part + 1)
                (src, hi, lo), cols = quarter(part)
                dve.tensor_tensor(lo[:, cols], src[:, cols], hi[:, cols].bitcast(F32), ALU.subtract)\
                    .then_inc(qk_done, 1)

            def scan(i, at, width, h, n):
                dve.wait_ge(z_read, PIECES * h + (n + 1))
                left = S - (i + 1) * P + at
                r = rest[i % RESTS]
                if at + width < (i + 1) * P:
                    dve.wait_ge(scanned, PIECES * h + n)
                backwards = r[:, left:left + width][:, ::-1]
                dve.tensor_tensor_scan(out=backwards, data0=backwards, data1=backwards,
                                       initial=r[:, left + width:left + width + 1], op0=ALU.mult,
                                       op1=ALU.bypass).then_inc(scanned, 1)

            def copy_lo(h, e, t):
                dve.wait_ge(hi_copied, STEPS * h + (t + 1))
                if e[0] == "V":
                    cols = slice(e[1] * CW, (e[1] + 1) * CW)
                    dve.tensor_tensor(v_lo[:, cols], t_bank(t)[:, :], v_hi[:, cols].bitcast(F32), ALU.subtract)\
                        .then_inc(lo_copied, 1)
                else:
                    n, c0 = product_of(e) % W_BUFS, max(0, e[2] - QT * e[1]) * P
                    dve.tensor_tensor(wT_lo[n][:, c0:], t_bank(t)[:, c0:], wT_hi[n][:, c0:].bitcast(F32),
                                      ALU.subtract).then_inc(lo_copied, 1)

            def body(h, last):
                for e, n in places(head_order(last)):
                    if e[0] == "W" and e[1] >= NT - QT:
                        scan(*e[1:], h, FIRST + n)
                    elif e[0] == "W":
                        scan(*e[1:], h + 1, FIRST + n - PIECES)
                    elif e[0] == "QK":
                        split_qk(h + 1, e[1])
                    elif e[0] in "VB":
                        copy_lo(h, e, n)
                    elif e[0] == "Y":
                        sup, m = e[1], e[1] % 2
                        dve.wait_ge(product, PRODUCTS * h + products_until(sup))
                        dve.wait_ge(zb_loaded[m], 32 * h + 16 * (sup // 2 + 1))
                        wait_past(dve, stored[m], 32 * h + 16 * (sup // 2))
                        dve.tensor_tensor(y[m][:, :], y_ps[sup % Y_BANKS][:, :], zb[m][:, :], ALU.mult).then_inc(y_done[m], 1)

            for n in range(RESTS):
                dve.memset(rest[n][:, S:S + 1], 1.0).then_inc(ones_set, 1)
            dve.wait_ge(ident_done, 1)
            dve.tensor_copy(ident_r[:, :], ident[:, :]).then_inc(consts, 1)
            dve.wait_ge(mask_done, 1)
            dve.tensor_copy(mask_r[:, :], mask[:, :]).then_inc(consts, 1)
            for part in range(len(SPLITS)):
                split_qk(0, part)
            for n, e in enumerate(early):
                scan(*e[1:], 0, n)
            per_head(dve, body)

        @block.tensor
        def _(pe):
            def logits(i, at, width, h, n):
                before = last_user(n, PIECES, Z_BANKS)
                if before >= 0 or not first_head(h):
                    pe.wait_ge(z_read, PIECES * h + (before + 1))
                qs = slice(i * P, (i + 1) * P)
                out, ks = z_ps[n % Z_BANKS][:, 0:width], slice(at, at + width)
                diagonal = at + width == (i + 1) * P
                pe.matmul(out, q_hi[:, qs], k_hi[:, ks], start=True, stop=False)
                pe.matmul(out, q_hi[:, qs], k_lo[:, ks], start=False, stop=False)
                mm = pe.matmul(out, q_lo[:, qs], k_hi[:, ks], start=False, stop=not diagonal)
                if diagonal:
                    mm = pe.matmul(z_ps[n % Z_BANKS][:, width - P:width], ident_r[:, :], mask_r[:, :],
                                   start=False, stop=True)
                mm.then_inc(z_full, 1)

            def body(h, last):
                for e, n in places(head_order(last)):
                    if e[0] == "Z" and e[1] >= NT - QT:
                        if e == z_pieces(NSUP - 1)[0]:
                            pe.wait_ge(qk_done, len(SPLITS) * h + len(SPLITS))
                        logits(*e[1:], h, FIRST + n)
                    elif e[0] == "Z":
                        sup = e[1] // QT
                        if e == z_pieces(sup)[0]:
                            pe.wait_ge(qk_done, len(SPLITS) * h + (len(SPLITS) + splits_for(sup)))
                        logits(*e[1:], h + 1, FIRST + n - PIECES)
                    elif e[0] in "VB":
                        copied(pe, h, last_user(n, STEPS, T_BANKS))
                        bank = t_bank(n)
                        if e == ("V", 0):
                            pe.wait_ge(v_loaded, 16 * h + 16)
                        for j in range(QT):
                            out = bank[:, j * P:(j + 1) * P]
                            if e[0] == "V":
                                at = (e[1] * QT + j) * P
                                ins = pe.transpose(out, v_in[:, at:at + P], ident[:, :])
                            elif e[2] <= QT * e[1] + j:
                                i, kt = QT * e[1] + j, e[2]
                                if kt == 0:
                                    pe.wait_ge(weighted, PIECES * h + pieces_before(i + 1))
                                ins = pe.transpose(out, slot[i][:, kt * P:(kt + 1) * P], ident[:, :])
                        ins.then_inc(turned, 1)
                    elif e[0] == "P":
                        _, sup, kt = e
                        bank = y_ps[sup % Y_BANKS]
                        c0 = max(0, kt - QT * sup) * P
                        copied(pe, h, kinds.index(("B", sup, kt)))
                        if kt == 0:
                            wait_past(pe, y_done[(sup - Y_BANKS) % 2], 2 * h + (sup - Y_BANKS) // 2 + 1)
                        ks, hi, lo = slice(kt * P, (kt + 1) * P), wT_hi[n % W_BUFS], wT_lo[n % W_BUFS]
                        pe.matmul(bank[:, c0:], v_hi[:, ks], hi[:, c0:], start=(kt == 0), stop=False)
                        pe.matmul(bank[:, c0:], v_hi[:, ks], lo[:, c0:], start=False, stop=False)
                        pe.matmul(bank[:, c0:], v_lo[:, ks], hi[:, c0:], start=False,
                                  stop=(('B', sup, kt) == b_steps(sup)[-1])).then_inc(product, 1)

            pe.wait_ge(consts, 2)
            for n, e in enumerate(early):
                if e == z_pieces(e[1] // QT)[0]:
                    pe.wait_ge(qk_done, splits_for(e[1] // QT))
                logits(*e[1:], 0, n)
            per_head(pe, body)


def merge_and_project_out(nc, x, w_o_sb, w_out, norm_final, out, s, carried):
    x_t = x.rearrange("a (t p) d -> (a t) p d", p=P)
    out_t = out.rearrange("a (t p) d -> (a t) p d", p=P)
    yb_k, gb_k, pa_k = (s[n].rearrange("(k p) s -> p k s", p=P) for n in ("yb_T", "gb_T", "pa_T"))
    HALVES = D // CW
    WF_AFTER = {3: 0, 6: 1, KT: 2, KT + 1: 3}
    with ExitStack() as memory:
        sc = Scope(nc, memory, "b")
        wo_hi, wo_lo, wf_hi, wf_lo = (sc.sb(n, [P, KT, D], F32R) for n in ("wo_hi", "wo_lo", "wf_hi", "wf_lo"))
        y_in = sc.sb("y_in", [P, KT, PW])
        y_hi = sc.sb("y_hi", [P, KT, PW], F32R)
        y_lo = sc.sb("y_lo", [P, KT, PW], F32R)
        gate = sc.sb("gate", [P, KT, PW])
        pa = carried.as_weights(2)
        m_hi = sc.sb("m_hi", [P, KT, PW], F32R)
        m_lo = sc.sb("m_lo", [P, KT, PW], F32R)
        x_sb = carried.as_tiles(0)
        o_sb = carried.as_tiles(1)
        gain = sc.sb("gain", [P, D])
        sq_sum, mean_sq, inv_rms = (sc.sb(n, [P, PT]) for n in ("sq_sum", "mean_sq", "inv_rms"))
        minus_half = sc.sb("minus_half", [P, 1])
        p_ps = [sc.ps(f"p_ps{n}", [P, CW]) for n in range(4)]
        acc = [sc.ps(f"acc{n}", [P, D]) for n in range(PT)]

        gain_loaded, half_set = sc.sem("gain_loaded"), sc.sem("half_set")
        w_loaded = sc.sem("w_loaded")
        w_hi_done, w_lo_done = sc.sem("w_hi_done"), sc.sem("w_lo_done")
        y_loaded, gate_loaded, pa_loaded = (sc.sem(n) for n in ("y_loaded", "gate_loaded", "pa_loaded"))
        y_hi_done, y_lo_done = sc.sem("y_hi_done"), sc.sem("y_lo_done")
        full, gated, merged, m_hi_done, m_lo_done = (
            sc.sem(n) for n in ("full", "gated", "merged", "m_hi_done", "m_lo_done"))
        x_loaded, full_out, summed, squared, mean_done, rms_done, o_done, stored = (
            sc.sems(n, PT) for n in ("x_loaded", "full_out", "summed", "squared", "mean_done", "rms_done",
                                     "o_done", "stored"))
        block = memory.enter_context(nc.Block())
        N_WO = D // WT
        buffer_of = [*range(N_CARRIED), *((n - N_CARRIED) % 2 for n in range(N_CARRIED, 2 * N_WO))]
        pieces = []
        for n in range(2 * N_WO):
            hi, lo = (wo_hi, wo_lo) if n < N_WO else (wf_hi, wf_lo)
            cols = slice(n % N_WO * WT, (n % N_WO + 1) * WT)
            loaded = (w_loaded, 16 * (n + 1 - N_CARRIED)) if n >= N_CARRIED else (carried.wo_b_loaded, 16 * N_CARRIED)
            pieces.append((carried.as_weights(buffer_of[n]), hi[:, :, cols], lo[:, :, cols], *loaded))

        @block.sync
        def _(sp):
            def snap(v):
                return v if isinstance(v, int) else sp.snap(v)

            def load_x(c, n, tile):
                wait_past(sp, o_done[n], c)
                sp.dma_start(x_sb[:, n], x_t[bass.ds(tile, 1)].rearrange("a p d -> p (a d)"))\
                    .then_inc(x_loaded[n], 16)

            def load_y(c, at):
                wait_past(sp, y_lo_done, c)
                sp.dma_start(y_in[:, :, :], yb_k[:, :, bass.ds(at, PW)]).then_inc(y_loaded, 16)

            def load_gate(c, at):
                wait_past(sp, m_lo_done, KT * c)
                sp.dma_start(gate[:, :, :], gb_k[:, :, bass.ds(at, PW)]).then_inc(gate_loaded, 16)

            def load_pa(c, at):
                wait_past(sp, merged, KT * c)
                sp.dma_start(pa[:, :, :], pa_k[:, :, bass.ds(at, PW)]).then_inc(pa_loaded, 16)

            def load_weights(n):
                if n > N_CARRIED:
                    sp.wait_ge(w_loaded, 16 * (n - N_CARRIED))
                before = max(m for m in range(n) if buffer_of[m] == buffer_of[n])
                sp.wait_ge(w_lo_done, before + 1)
                sp.dma_start(pieces[n][0], w_piece(w_o_sb if n < N_WO else w_out, n % N_WO))\
                    .then_inc(w_loaded, 16)

            load_y(0, 0)
            load_weights(N_CARRIED)
            load_gate(0, 0)
            sp.dma_start(gain[:, :], norm_final.unsqueeze(0).to_broadcast([P, D])).then_inc(gain_loaded, 16)
            sp.wait_ge(w_lo_done, N_CARRIED)
            load_pa(0, 0)
            for n in range(N_WO, 2 * N_WO):
                load_weights(n)
            sp.wait_ge(w_lo_done, 2 * N_WO)
            for n in range(PT):
                load_x(0, n, n)

            with sp.Fori(1, NPW) as c:
                at, tiles = snap(c * PW), [snap(PT * c + n) for n in range(PT)]
                load_y(c, at)
                load_gate(c, at)
                load_pa(c, at)
                for n in range(PT):
                    load_x(c, n, tiles[n])

        @block.gpsimd
        def _(pool):
            pool.memset(minus_half[:, :], -0.5).then_inc(half_set, 1)
            pool.wait_ge(half_set, 1)
            with pool.Fori(0, NPW) as c:
                for n in range(PT):
                    pool.wait_ge(mean_done[n], c + 1)
                    pool.tensor_tensor(inv_rms[:, n:n + 1], mean_sq[:, n:n + 1], minus_half[:, :],
                                       ALU.pow).then_inc(rms_done[n], 1)

        @block.scalar
        def _(act):
            def round_y(c):
                act.wait_ge(y_loaded, 16 * c + 16)
                wait_past(act, full, KT * c)
                act.activation(y_hi[:, :, :], y_in[:, :, :], ACT.Copy).then_inc(y_hi_done, 1)

            def body(c, last):
                for k in range(KT):
                    act.wait_ge(merged, KT * c + (k + 1))
                    if k == 0:
                        for n in range(PT):
                            wait_past(act, full_out[n], c)
                    act.activation(m_hi[:, k], gate[:, k], ACT.Copy).then_inc(m_hi_done, 1)
                    if isinstance(c, int) and c == 0 and k in WF_AFTER:
                        round_weights(act, pieces, N_WO + WF_AFTER[k], w_hi_done)
                if isinstance(c, int) and c == 0:
                    for k in (KT, KT + 1):
                        round_weights(act, pieces, N_WO + WF_AFTER[k], w_hi_done)
                    act.wait_ge(w_lo_done, 2 * N_WO)
                if not last:
                    round_y(c + 1)
                for n in range(PT):
                    act.wait_ge(summed[n], c + 1)
                    wait_past(act, stored[n], 16 * c)
                    act.activation(o_sb[:, n], x_sb[:, n], ACT.Square, accum_out=sq_sum[:, n:n + 1])\
                        .then_inc(squared[n], 1)
                for n in range(PT):
                    act.wait_ge(o_done[n], c + 1)
                    act.dma_start(out_t[bass.ds(PT * c + n, 1)].rearrange("a p d -> p (a d)"), o_sb[:, n])\
                        .then_inc(stored[n], 16)

            for n in range(N_WO):
                if n == N_CARRIED:
                    round_y(0)
                round_weights(act, pieces, n, w_hi_done)
            body(0, False)
            with act.Fori(1, NPW - 1) as c:
                body(c, False)
            body(NPW - 1, True)
            for n in range(PT):
                act.wait_ge(stored[n], 16 * NPW)

        @block.vector
        def _(dve):
            def rest_y(c):
                dve.wait_ge(y_hi_done, c + 1)
                dve.tensor_tensor(y_lo[:, :, :], y_in[:, :, :], y_hi[:, :, :].bitcast(F32), ALU.subtract)\
                    .then_inc(y_lo_done, 1)

            def body(c, last):
                def rest_m(k):
                    dve.wait_ge(m_hi_done, KT * c + (k + 1))
                    dve.tensor_tensor(m_lo[:, k], gate[:, k], m_hi[:, k].bitcast(F32), ALU.subtract)\
                        .then_inc(m_lo_done, 1)

                dve.wait_ge(gate_loaded, 16 * c + 16)
                dve.wait_ge(pa_loaded, 16 * c + 16)
                for k in range(KT):
                    dve.wait_ge(full, KT * c + (k + 1))
                    dve.tensor_tensor(gate[:, k], p_ps[k % 4][:, 0:PW], gate[:, k], ALU.mult).then_inc(gated, 1)
                    dve.wait_ge(gated, KT * c + (k + 1))
                    dve.tensor_tensor(gate[:, k], gate[:, k], pa[:, k], ALU.add).then_inc(merged, 1)
                    if k >= 1:
                        rest_m(k - 1)
                        if isinstance(c, int) and c == 0 and k - 1 in WF_AFTER:
                            rest_weights(dve, pieces, N_WO + WF_AFTER[k - 1], w_hi_done, w_lo_done)
                rest_m(KT - 1)
                if isinstance(c, int) and c == 0:
                    for k in (KT, KT + 1):
                        rest_weights(dve, pieces, N_WO + WF_AFTER[k], w_hi_done, w_lo_done)
                if not last:
                    rest_y(c + 1)
                for n in range(PT):
                    dve.wait_ge(x_loaded[n], 16 * c + 16)
                    dve.wait_ge(full_out[n], c + 1)
                    dve.tensor_tensor(x_sb[:, n], acc[n][:, :], x_sb[:, n], ALU.add).then_inc(summed[n], 1)
                    dve.wait_ge(squared[n], c + 1)
                    dve.tensor_scalar(mean_sq[:, n:n + 1], sq_sum[:, n:n + 1], 1.0 / D, EPS, ALU.mult,
                                      ALU.add).then_inc(mean_done[n], 1)
                    dve.wait_ge(rms_done[n], c + 1)
                    dve.scalar_tensor_tensor(o_sb[:, n], x_sb[:, n], inv_rms[:, n:n + 1], gain[:, :],
                                             ALU.mult, ALU.mult).then_inc(o_done[n], 1)

            for n in range(N_WO):
                if n == N_CARRIED:
                    rest_y(0)
                rest_weights(dve, pieces, n, w_hi_done, w_lo_done)
            dve.wait_ge(gain_loaded, 16)
            body(0, False)
            with dve.Fori(1, NPW - 1) as c:
                body(c, False)
            body(NPW - 1, True)

        @block.tensor
        def _(pe):
            def body(c):
                first = isinstance(c, int)
                pe.wait_ge(y_lo_done, c + 1)
                for k in range(KT):
                    if first and k % 2 == 0:
                        pe.wait_ge(w_lo_done, k // 2 + 1)
                    if not (first and k < 4):
                        pe.wait_ge(gated, KT * c + (k - 3))
                    out_, ks = p_ps[k % 4][:, 0:PW], slice(k * P, (k + 1) * P)
                    for j in range(KT):
                        pe.matmul(out_, wo_hi[:, j, ks], y_hi[:, j], start=(j == 0), stop=False)
                        pe.matmul(out_, wo_hi[:, j, ks], y_lo[:, j], start=False, stop=False)
                        mm = pe.matmul(out_, wo_lo[:, j, ks], y_hi[:, j], start=False, stop=(j == KT - 1))
                    mm.then_inc(full, 1)
                order = [(n, half) for half in range(HALVES) for n in range(PT)] if first else \
                    [(n, half) for n in range(PT) for half in range(HALVES)]
                for n, half in order:
                    if half == 0:
                        wait_past(pe, summed[n], c)
                    if first and n == 0:
                        pe.wait_ge(w_lo_done, N_WO + (half + 1) * N_WO // HALVES)
                    ts, cols = slice(n * P, (n + 1) * P), slice(half * CW, (half + 1) * CW)
                    for k in range(KT):
                        if (n, half) == (0, 0):
                            pe.wait_ge(m_lo_done, KT * c + (k + 1))
                        pe.matmul(acc[n][:, cols], m_hi[:, k, ts], wf_hi[:, k, cols], start=(k == 0), stop=False)
                        pe.matmul(acc[n][:, cols], m_hi[:, k, ts], wf_lo[:, k, cols], start=False, stop=False)
                        mm = pe.matmul(acc[n][:, cols], m_lo[:, k, ts], wf_hi[:, k, cols], start=False,
                                       stop=(k == KT - 1))
                    if half == HALVES - 1:
                        mm.then_inc(full_out[n], 1)

            turns_from_first(pe, NPW, body)


class Carried:

    def __init__(self, sc):
        self.sc = sc
        self.buffer = []
        self.wo_a_loaded = sc.sem("wo_a_loaded")
        self.q_k_loaded = sc.sem("q_k_loaded")
        self.v_loaded = sc.sem("v_loaded")
        self.wo_b_loaded = sc.sem("wo_b_loaded")

    def add(self):
        self.buffer.append(self.sc.sb(f"buffer{len(self.buffer)}", [P, S]))

    def as_tiles(self, n):
        return self.buffer[n][:, :].rearrange("p (t d) -> p t d", t=2)

    def as_weights(self, n):
        return self.buffer[n][:, :].rearrange("p (k f) -> p k f", k=KT)


def hybrid_block(nc, x, norm_in, w_in, norm_v, w_s, b_s, w_o_gmlp, w_o_sb, w_out, norm_final, out):
    s = {n: nc.dram_tensor(n, [D, S], F32, kind="Internal").ap()
         for n in ("uz_T", "va_T", "q_T", "k_T", "vb_T", "zb_T", "ga_T", "gb_T", "pa_T", "yb_T")}
    with ExitStack() as memory:
        sc = Scope(nc, memory, "carried")
        carried = Carried(sc)
        carried.add()
        norm_and_project(nc, x, norm_in, w_in, w_o_gmlp, s, carried)
        carried.add()
        carried.add()
        gate_and_project_a(nc, norm_v, w_s, b_s, w_o_gmlp, s, carried)
        attention(nc, w_o_sb, s, carried)
        merge_and_project_out(nc, x, w_o_sb, w_out, norm_final, out, s, carried)
        sc.clear()


_INS = ["x", "norm_in", "w_in", "norm_v", "w_s", "b_s", "w_o_gmlp", "w_o_sb", "w_out", "norm_final"]


def kernel(**inputs):
    import numpy as np
    import concourse.bacc as bacc
    from concourse.bass_utils import run_bass_kernel_spmd

    nc = bacc.Bacc("TRN2", target_bir_lowering=False, num_devices=1)
    arrays, args = {}, []
    for name in _INS:
        a = np.ascontiguousarray(inputs[name])
        arrays[f"in_{name}"] = a
        args.append(nc.dram_tensor(f"in_{name}", a.shape, mybir.dt.from_np(a.dtype), kind="ExternalInput").ap())
    out = nc.dram_tensor("out", [1, S, D], F32, kind="ExternalOutput").ap()
    hybrid_block(nc, *args, out)
    r = run_bass_kernel_spmd(nc, [arrays], core_ids=[0])
    return r.results[0]["out"]
```
